# Optimizing a Trainium2 kernel written in Bass

```python
import jax, jax.numpy as jnp
from jax import lax
import numpy as np

D_MODEL = 1024
BATCH = 1
SEQ = 256
DEPTH = 2

CONV_DIM = 512
CONV_WIDTH = 31
SB_HEADS = 8
SB_HEAD_DIM = 64
SB_DIM = SB_HEADS * SB_HEAD_DIM
SB_BLOCK = 128
GLA_HEADS = 4
GLA_DK = 128
GLA_DV = 128
GLA_KDIM = GLA_HEADS * GLA_DK
GLA_VDIM = GLA_HEADS * GLA_DV
GLA_GATE_RANK = 16
GLA_GATE_TAU = 16.0
GLA_CHUNK = 64
N_BRANCH = 3
IN_SIZES = (2 * CONV_DIM, 3 * SB_DIM, GLA_KDIM, GLA_KDIM, GLA_VDIM, GLA_VDIM, GLA_GATE_RANK, N_BRANCH * D_MODEL)
IN_COLS = 2 * CONV_DIM + 3 * SB_DIM + 2 * GLA_KDIM + 2 * GLA_VDIM + GLA_GATE_RANK + N_BRANCH * D_MODEL
D_FF = 2816
N_EXPERTS = 8
TOP_K = 2
D_FF_EXPERT = 3584
N_ADA = 6
EPS = 1e-6

kernel_name = 'hybrid_gated_conv_stickbreak_gla_moe'

def rms_norm(x, g):
    xf = x.astype(jnp.float32)
    y = xf * lax.rsqrt(jnp.mean(xf * xf, axis=-1, keepdims=True) + EPS)
    return (y * g.astype(jnp.float32)).astype(x.dtype)

def layer_norm(x, g, b):
    xf = x.astype(jnp.float32)
    mu = jnp.mean(xf, axis=-1, keepdims=True)
    var = jnp.mean(jnp.square(xf - mu), axis=-1, keepdims=True)
    y = (xf - mu) * lax.rsqrt(var + EPS)
    return (y * g.astype(jnp.float32) + b.astype(jnp.float32)).astype(x.dtype)

def heads(t, n):
    return t.reshape(t.shape[0], t.shape[1], n, -1).transpose(0, 2, 1, 3)

def conformer_conv(u, w_dw, b_dw, ln_g, ln_b, w_out):
    a, g = jnp.split(u, 2, axis=-1)
    y = a * jax.nn.sigmoid(g)
    y = lax.conv_general_dilated(
        y, w_dw[:, None, :].astype(y.dtype), window_strides=(1,),
        padding=((CONV_WIDTH - 1, 0),),
        dimension_numbers=('NWC', 'WIO', 'NWC'),
        feature_group_count=CONV_DIM) + b_dw
    y = jax.nn.silu(layer_norm(y, ln_g, ln_b))
    return y @ w_out

def stick_breaking_attention(q, k, v):
    scale = SB_HEAD_DIM ** -0.5
    n_blocks = q.shape[2] // SB_BLOCK
    outs = []
    for i in range(n_blocks):
        t0 = i * SB_BLOCK
        t1 = t0 + SB_BLOCK
        qb = q[:, :, t0:t1]
        kb = k[:, :, :t1]
        vb = v[:, :, :t1]
        z = jnp.einsum('bhtd,bhsd->bhts', qb, kb).astype(jnp.float32) * scale
        t_idx = t0 + jnp.arange(SB_BLOCK)[:, None]
        s_idx = jnp.arange(t1)[None, :]
        causal = s_idx < t_idx
        log_beta = jax.nn.log_sigmoid(z)
        log_keep = jnp.where(causal, jax.nn.log_sigmoid(-z), 0.0)
        log_rest = lax.cumsum(log_keep, axis=3, reverse=True) - log_keep
        att = jnp.where(causal, jnp.exp(log_beta + log_rest), 0.0)
        outs.append(jnp.einsum('bhts,bhsd->bhtd', att.astype(v.dtype), vb))
    return jnp.concatenate(outs, axis=2)

def gla_chunked(q, k, v, log_a):
    B, H, S, dk = q.shape
    dv = v.shape[-1]
    n = S // GLA_CHUNK
    q = q.reshape(B, H, n, GLA_CHUNK, dk)
    k = k.reshape(B, H, n, GLA_CHUNK, dk)
    v = v.reshape(B, H, n, GLA_CHUNK, dv)
    log_a = log_a.reshape(B, H, n, GLA_CHUNK, dk)
    b = jnp.cumsum(log_a, axis=3)
    b_last = b[:, :, :, -1:, :]
    q_dec = q * jnp.exp(b)
    k_inv = k * jnp.exp(-b)
    k_end = k * jnp.exp(b_last - b)
    mask = jnp.tril(jnp.ones((GLA_CHUNK, GLA_CHUNK), dtype=bool))
    scores = jnp.where(mask, jnp.einsum('bhnck,bhnsk->bhncs', q_dec, k_inv), 0.0)
    o_intra = jnp.einsum('bhncs,bhnsv->bhncv', scores, v)
    d_state = jnp.einsum('bhnsk,bhnsv->bhnkv', k_end, v)
    decay = jnp.exp(b_last[:, :, :, 0, :])

    def step(state, inp):
        dec, ds = inp
        return dec[..., None] * state + ds, state

    s0 = jnp.zeros((B, H, dk, dv), jnp.float32)
    _, s_before = lax.scan(step, s0, (jnp.moveaxis(decay, 2, 0), jnp.moveaxis(d_state, 2, 0)))
    s_before = jnp.moveaxis(s_before, 0, 2)
    o_inter = jnp.einsum('bhnck,bhnkv->bhncv', q_dec, s_before)
    return (o_intra + o_inter).reshape(B, H, S, dv)

def hybrid_mixer(h, w_in, gla_a2, gla_a_b, conv_dw, conv_dw_b, conv_ln_g, conv_ln_b,
                 gla_norm_g, w_conv_out, w_sb_out, w_gla_out, w_o):
    B, S, _ = h.shape
    z = h @ w_in
    offs = []
    acc = 0
    for n in IN_SIZES[:-1]:
        acc += n
        offs.append(acc)
    u_conv, sb_qkv, gq, gk, gv, gg, g_lr, gates = jnp.split(z, offs, axis=-1)
    y_a = conformer_conv(u_conv, conv_dw, conv_dw_b, conv_ln_g, conv_ln_b, w_conv_out)
    sq, sk, sv = jnp.split(sb_qkv, 3, axis=-1)
    o_b = stick_breaking_attention(heads(sq, SB_HEADS), heads(sk, SB_HEADS), heads(sv, SB_HEADS))
    y_b = o_b.transpose(0, 2, 1, 3).reshape(B, S, SB_DIM) @ w_sb_out
    log_a = jax.nn.log_sigmoid((g_lr @ gla_a2 + gla_a_b).astype(jnp.float32)) / GLA_GATE_TAU
    o_c = gla_chunked(heads(gq, GLA_HEADS).astype(jnp.float32) * (GLA_DK ** -0.5),
                      heads(gk, GLA_HEADS).astype(jnp.float32),
                      heads(gv, GLA_HEADS).astype(jnp.float32),
                      heads(log_a, GLA_HEADS))
    o_c = rms_norm(o_c.transpose(0, 2, 1, 3), gla_norm_g.reshape(GLA_HEADS, GLA_DV)).astype(h.dtype)
    y_c = (o_c.reshape(B, S, GLA_VDIM) * jax.nn.silu(gg)) @ w_gla_out
    g_a, g_b, g_c = jnp.split(jax.nn.sigmoid(gates), N_BRANCH, axis=-1)
    return (g_a * y_a + g_b * y_b + g_c * y_c) @ w_o

def swiglu(h, w_gate, w_up, w_down):
    return (jax.nn.silu(h @ w_gate) * (h @ w_up)) @ w_down

def moe_swiglu(h, router_w, w_gate, w_up, w_down):
    logits = (h @ router_w).astype(jnp.float32)
    top_val, top_idx = lax.top_k(logits, TOP_K)
    probs = jax.nn.softmax(top_val, axis=-1)
    combine = jnp.sum(jax.nn.one_hot(top_idx, N_EXPERTS, dtype=jnp.float32) * probs[..., None], axis=-2)
    out = jnp.zeros_like(h)
    for e in range(N_EXPERTS):
        out = out + combine[..., e:e + 1].astype(h.dtype) * swiglu(h, w_gate[e], w_up[e], w_down[e])
    return out

def setup_inputs(seed: int = 0) -> dict:
    key = jax.random.key(seed)
    ks = iter(jax.random.split(key, 40))

    def nrm(shape, scale):
        return jax.random.normal(next(ks), shape, jnp.float32) * scale

    def gain(shape):
        return 1.0 + nrm(shape, 0.02)

    L = DEPTH
    ND = (DEPTH + 1) // 2
    NM = DEPTH // 2
    return {
        'x': nrm((BATCH, SEQ, D_MODEL), 1.0),
        'c': nrm((BATCH, D_MODEL), 1.0),
        'ada_w': nrm((L, D_MODEL, N_ADA * D_MODEL), 0.5 * D_MODEL ** -0.5),
        'ada_b': nrm((L, N_ADA * D_MODEL), 0.02),
        'mix_pre_g': gain((L, D_MODEL)),
        'mix_post_g': gain((L, D_MODEL)),
        'ffn_pre_g': gain((L, D_MODEL)),
        'ffn_post_g': gain((L, D_MODEL)),
        'w_in': nrm((L, D_MODEL, IN_COLS), D_MODEL ** -0.5),
        'gla_a2': nrm((L, GLA_GATE_RANK, GLA_KDIM), GLA_GATE_RANK ** -0.5),
        'gla_a_b': nrm((L, GLA_KDIM), 0.02),
        'conv_dw': nrm((L, CONV_WIDTH, CONV_DIM), CONV_WIDTH ** -0.5),
        'conv_dw_b': nrm((L, CONV_DIM), 0.02),
        'conv_ln_g': gain((L, CONV_DIM)),
        'conv_ln_b': nrm((L, CONV_DIM), 0.02),
        'gla_norm_g': gain((L, GLA_VDIM)),
        'w_conv_out': nrm((L, CONV_DIM, D_MODEL), CONV_DIM ** -0.5),
        'w_sb_out': nrm((L, SB_DIM, D_MODEL), SB_DIM ** -0.5),
        'w_gla_out': nrm((L, GLA_VDIM, D_MODEL), GLA_VDIM ** -0.5),
        'w_o': nrm((L, D_MODEL, D_MODEL), D_MODEL ** -0.5),
        'ffn_w_gate': nrm((ND, D_MODEL, D_FF), D_MODEL ** -0.5),
        'ffn_w_up': nrm((ND, D_MODEL, D_FF), D_MODEL ** -0.5),
        'ffn_w_down': nrm((ND, D_FF, D_MODEL), D_FF ** -0.5),
        'router_w': nrm((NM, D_MODEL, N_EXPERTS), D_MODEL ** -0.5),
        'moe_w_gate': nrm((NM, N_EXPERTS, D_MODEL, D_FF_EXPERT), D_MODEL ** -0.5),
        'moe_w_up': nrm((NM, N_EXPERTS, D_MODEL, D_FF_EXPERT), D_MODEL ** -0.5),
        'moe_w_down': nrm((NM, N_EXPERTS, D_FF_EXPERT, D_MODEL), D_FF_EXPERT ** -0.5),
    }

def reference(x, c, ada_w, ada_b, mix_pre_g, mix_post_g, ffn_pre_g, ffn_post_g, w_in,
              gla_a2, gla_a_b, conv_dw, conv_dw_b, conv_ln_g, conv_ln_b, gla_norm_g,
              w_conv_out, w_sb_out, w_gla_out, w_o, ffn_w_gate, ffn_w_up, ffn_w_down,
              router_w, moe_w_gate, moe_w_up, moe_w_down):
    cond = jax.nn.silu(c)
    for l in range(DEPTH):
        mod = (cond @ ada_w[l] + ada_b[l])[:, None, :]
        sh_m, sc_m, g_m, sh_f, sc_f, g_f = jnp.split(mod, N_ADA, axis=-1)
        h = rms_norm(x, mix_pre_g[l]) * (1 + sc_m) + sh_m
        y = hybrid_mixer(h, w_in[l], gla_a2[l], gla_a_b[l], conv_dw[l], conv_dw_b[l],
                         conv_ln_g[l], conv_ln_b[l], gla_norm_g[l], w_conv_out[l],
                         w_sb_out[l], w_gla_out[l], w_o[l])
        x = x + g_m * rms_norm(y, mix_post_g[l])
        h = rms_norm(x, ffn_pre_g[l]) * (1 + sc_f) + sh_f
        j = l // 2
        if l % 2 == 0:
            y = swiglu(h, ffn_w_gate[j], ffn_w_up[j], ffn_w_down[j])
        else:
            y = moe_swiglu(h, router_w[j], moe_w_gate[j], moe_w_up[j], moe_w_down[j])
        x = x + g_f * rms_norm(y, ffn_post_g[l])
    return x


_drawn_inputs = setup_inputs


def setup_inputs(seed=0):
    import zlib

    import numpy as np

    out = dict(_drawn_inputs(seed))
    spreads = {}
    factors = {'mix_post_g': 2.83,
     'ffn_post_g': 4.062,
     'gla_a_b': 8.0,
     'conv_dw_b': 4.358,
     'conv_ln_g': 3.386,
     'gla_norm_g': 8.0}
    for name, (base, spread) in spreads.items():
        noise = np.random.default_rng([zlib.crc32(name.encode()), seed]).standard_normal(out[name].shape)
        drawn = base * np.exp(spread * noise) if base else spread * noise
        out[name] = __import__('jax').numpy.asarray(drawn.astype(out[name].dtype))
    for name, factor in factors.items():
        out[name] = (out[name] * factor).astype(out[name].dtype)
    return out
```

```python
from contextlib import ExitStack

import concourse.bass as bass
import numpy as np
from concourse import mybir

F32 = mybir.dt.float32
F32R = mybir.dt.float32r
I32 = mybir.dt.int32
U32 = mybir.dt.uint32
ALU = mybir.AluOpType
ACT = mybir.ActivationFunctionType

P = 128
D = 1024
T = 256
DEPTH = 2
KC = D // P
CONV = 512
TAPS = 31
SB_HEADS, SB_DH = 8, 64
GLA_HEADS, GLA_D = 4, 128
CH = 64
RANK = 16
D_FF = 2816
N_EXP = 8
D_FFE = 3584
EPS = 1e-6

WORDS = 2048
RAW = 6
SPLIT = 2
LAG = 2
WBANKS = 3
FT = D_FFE // 512
EU = 6 * FT

Z_UNITS = 18
G_UNITS = 12
PAIRS = D_FF // 256

O_SB = 2 * CONV
O_GLA = O_SB + 3 * 512
O_LR = O_GLA + 4 * 512
O_GATES = O_LR + RANK


def z_columns():
    cols = [(CONV, False), (0, False), (CONV + 256, False), (256, False)]
    for part in range(3):
        cols += [(O_SB + 512 * part + 256 * h, part == 2) for h in range(2)]
    for part in range(4):
        cols += [(O_GLA + 512 * part + 256 * h, part == 2) for h in range(2)]
    cols += [(O_GATES + 256 * u, False) for u in range(G_UNITS)]
    return cols


def plan():
    units = [("ada", 0, 0, k) for k in range(KC)]
    for layer in range(DEPTH):
        later = [("ada", 0, g, k) for g in (1, 2) for k in range(KC)] if layer == 0 else []
        for u in range(Z_UNITS + G_UNITS):
            units.append(("z", layer, u, 0))
            if later:
                units.append(later.pop(0))
        units += [("out", layer, b, h) for b in (1, 0, 2) for h in range(2)]
        units += [("wo", layer, q, 0) for q in range(4)]
        if layer == 0:
            later = [("ada", 1, g, k) for g in range(3) for k in range(KC)]
            for t in range(PAIRS + 1):
                if t < PAIRS:
                    units += [("gate", 0, t, 0)] + later[:1] + [("up", 0, t, 0)] + later[1:2]
                    later = later[2:]
                if t:
                    units += [("down", 0, t - 1, 0)] + later[:1]
                    later = later[1:]
    return units


PLAN = plan()
N_UNITS = len(PLAN)
W_UNITS = [u for u in PLAN if u[0] != "ada"]
N_W = len(W_UNITS)
POS = {u: n for n, u in enumerate(PLAN)}
WPOS = {u: n for n, u in enumerate(W_UNITS)}

SLOT, FREED = {}, {}
_last = {}
for _w, _u in enumerate(W_UNITS):
    _slots = SPLIT + (_u[0] in ("gate", "up", "down"))
    SLOT[_u] = _w % _slots
    FREED[_u] = _last.get(SLOT[_u], -1) + 1
    _last[SLOT[_u]] = _w

VECS = {}
_at = 0
for _name, _n in (("mix_pre_g", 8), ("mix_post_g", 8), ("ffn_pre_g", 8), ("ffn_post_g", 8),
                  ("ada_b", 48), ("gla_a_b", 4), ("conv_dw_b", 4), ("conv_ln_g", 4),
                  ("conv_ln_b", 4), ("gla_norm_g", 4), ("conv_dw", 4 * TAPS)):
    VECS[_name] = (_at, _n)
    _at += _n
V_LAYER = _at
N_VEC = DEPTH * V_LAYER + KC

A_X = 0
A_H = A_X + 2048
A_GATES = A_H + 2048
A_Y = A_GATES + 6144
YW = TAPS - 1 + T
A_SQ = A_Y + 4 * YW
A_SK = A_SQ + 1024
A_SV = A_SK + 1024
A_GQ = A_SV + 1024
A_GK = A_GQ + 1024
A_GV = A_GK + 1024
A_GG = A_GV + 1024
A_ST = A_GG + 1024
A_CONST = A_ST + 2048
C_ID, C_ONES, C_LNEG, C_NEG = (A_CONST + P * i for i in range(4))
C_RS = A_CONST + 4 * P
C_RT = C_RS + T
C_MOD = C_RT + T
C_VEC = C_MOD + DEPTH * 80
C_COND = C_VEC + N_VEC
C_DEC = C_COND + KC
C_EPS = C_DEC + 16
A_END = C_EPS + 8


def program(nc, x_t, vecs, glr_w, a2, router, stream, experts, out_t):
    with ExitStack() as ctx:
        def sb(name, shape, dt=F32):
            return ctx.enter_context(nc.sbuf_tensor(name, shape, dt))

        def sem(name):
            return ctx.enter_context(nc.semaphore(name))

        raw = sb("raw", [P, RAW, WORDS])
        w_hi2 = sb("w_hi", [P, SPLIT, WORDS], F32R)
        w_lo2 = sb("w_lo", [P, SPLIT, WORDS], F32R)
        ar = sb("arena", [P, A_END])
        acts = sb("acts", [P, 10240], F32R)
        w_hi = [w_hi2[:, 0, :], w_hi2[:, 1, :], acts[:, 6144:8192]]
        w_lo = [w_lo2[:, 0, :], w_lo2[:, 1, :], acts[:, 8192:10240]]
        ints = sb("ints", [P, 24], I32)
        bank = [ctx.enter_context(nc.psum_tensor(f"bank{i}", [P, 512], F32)) for i in range(8)]
        WB = bank[0:3]
        Z = bank[3:5]
        O = bank[5:7]
        M = bank[7]

        def area(at, *dims):
            n = int(np.prod(dims))
            v = ar[:, at:at + n]
            if len(dims) == 2:
                return v.rearrange("p (a b) -> p a b", a=dims[0])
            if len(dims) == 3:
                return v.rearrange("p (a b c) -> p a b c", a=dims[0], b=dims[1])
            return v

        def split_area(at, *dims):
            n = int(np.prod(dims))
            if len(dims) == 1:
                return acts[:, at:at + n]
            return acts[:, at:at + n].rearrange("p (a b) -> p a b", a=dims[0])

        def f32(ap):
            return ap.bitcast(F32)

        x = area(A_X, KC, T)
        hf = area(A_H, KC, T)
        gates = area(A_GATES, 24, T)
        ada_acc = {(0, 0): area(A_GATES, 2048), (0, 1): area(A_GATES, 2048),
                   (0, 2): area(A_GATES + 2048, 2048), (1, 0): area(A_GATES + 4096, 2048),
                   (1, 1): area(A_GQ, 2048), (1, 2): area(A_GV, 2048)}
        y = area(A_GATES, KC, T)
        squares = area(A_GATES + 2048, KC, T)
        wglr = area(A_GATES + 4096, KC, RANK)
        a2_sb = area(A_GATES + 4096 + 128, 512)
        glr = area(A_GATES + 4096 + 640, T)
        ypad = area(A_Y, 4, YW)
        sq, sk, sv = area(A_SQ, 4, T), area(A_SK, 4, T), area(A_SV, 2, 512)
        gq, gk, gv, gg = area(A_GQ, 4, T), area(A_GK, 4, T), area(A_GV, 2, 512), area(A_GG, 4, T)
        conv_acc, conv_tmp = area(A_H, 4, T), area(A_H + 1024, 4, T)
        sig = area(A_ST, 2, T)
        stick_e = [area(A_ST + 512 * i, 2, T) for i in range(2)]
        stick_s = [area(A_ST + 1024 + 512 * i, 2, T) for i in range(2)]
        cum, gap, e_in, e_out = area(A_SQ, 4, T), area(A_SK, 4, T), area(A_SV, 4, T), area(A_ST, 4, T)
        ket, s_t = area(A_GK, 1024), area(A_GQ, 1024)
        states = [area(A_SQ, 512), area(A_SQ + 512, 512), area(A_ST + 1024, 512)]
        gla_o, gla_sq, gla_rs = area(A_SK, 4, T), area(A_ST, 4, T), area(A_SQ, 4, T)
        ident, ones = area(C_ID, P), area(C_ONES, P)
        l_neg, neg = area(C_LNEG, P), area(C_NEG, P)
        rs, rt = area(C_RS, T), area(C_RT, T)
        cond = area(C_COND, KC)
        decay = area(C_DEC, 4, 4)
        eps = area(C_EPS, 8)[:, 0:1]

        def mod(layer, i):
            at = C_MOD + 80 * layer + 8 * i
            return ar[:, at:at + 8]
        SH_M, SC_M, G_M, SH_F, SC_F, G_F, A_M, P_M, A_F, P_F = range(10)

        def vec(layer, name):
            at, n = VECS[name]
            at += C_VEC + V_LAYER * layer
            return ar[:, at:at + n]

        h_hi, h_lo = split_area(0, KC, T), split_area(2048, KC, T)
        br_hi = [split_area(4096 + 2048 * b, 4, T) for b in range(3)]
        br_lo = [split_area(4096 + 2048 * b + 1024, 4, T) for b in range(3)]
        ff_hi = [split_area(4096 + 1024 * b, 2, T) for b in range(2)]
        ff_lo = [split_area(4096 + 1024 * b + 512, 2, T) for b in range(2)]
        silu_g = [area(A_Y, 2, T), area(A_Y + 512, 2, T)]
        prod = [area(A_SQ, 2, T), area(A_SQ + 512, 2, T)]

        def bcast(row, n):
            return row.unsqueeze(1).to_broadcast([P, n, T])

        h_tok = area(A_GATES, 2 * D)
        moe_y = area(A_GATES + 2048, KC * T)
        y_e = area(A_GATES + 4096, D)
        silu_e = [area(A_GATES + 5120 + 512 * i, 512) for i in range(2)]
        act_e = [area(A_SQ + 512 * i, 512) for i in range(2)]
        sel, sel_w, sel_t = area(A_SK, T), area(A_SK + 256, T), area(A_SK + 512, T)
        iota, tril = area(A_SK + 768, P), area(A_SK + 896, P)
        logits, top = area(A_GQ, 16), area(A_GQ + 16, 2, 8)
        index_f, iota8 = area(A_GQ + 32, 2, 8), area(A_GQ + 48, 8)
        pick, pick_f = area(A_GQ + 56, 2, 8), area(A_GQ + 56, 16)
        comb, comb_f = area(A_GQ + 72, 2, 8), area(A_GQ + 72, 16)
        places, chosen, weights = (area(A_GQ + 512 + 32 * i, 2, 16) for i in range(3))
        places_f, chosen_f, weights_f = (area(A_GQ + 512 + 32 * i, 32) for i in range(3))
        column_f = area(A_GQ + 608, 12)
        prob, pick2 = area(A_GQ + 120, 2, 2), area(A_GQ + 124, 2, 8)
        over, place8 = area(A_GQ + 140, 8), area(A_GQ + 148, 8)
        list_f, hits = area(A_GQ + 156, 8), area(A_GQ + 164, 8)
        router_sb = area(A_GQ + 256, KC, N_EXP)
        index = sb("index", [P, 2, 8], U32)
        xe_hi, xe_lo = split_area(0, KC * P), split_area(1024, KC * P)
        ae_hi = [split_area(4096 + 1024 * b, 512) for b in range(2)]
        ae_lo = [split_area(4096 + 1024 * b + 512, 512) for b in range(2)]
        merged = area(A_H, KC, T)

        def flat(buffer):
            return buffer.rearrange("p a b -> p (a b)")[:, 0:384]

        SCATTER = (bank[2], bank[3], bank[7], bank[4])
        FB = Z + O
        ADA_TURN = (3, 6, 9)

        loaded = [sem(f"unit_loaded_{i}") for i in range(RAW)]
        hi_written = sem("hi_written")
        lo_written = sem("lo_written")
        released = sem("raw_slot_released")
        consumed = sem("unit_consumed")
        bank_read = [sem(f"bank_read_{i}") for i in range(WBANKS)]
        x_loaded, vec_loaded, lr_loaded = sem("x_loaded"), sem("vectors_loaded"), sem("low_rank_loaded")
        router_loaded = sem("router_loaded")
        consts, pad_zeroed = sem("constants_written"), sem("pad_zeroed")
        cond_ready = sem("cond_ready")
        ada_summed, ada_reduced, mods_ready = sem("ada_summed"), sem("ada_reduced"), sem("mods_ready")
        dve_step, act_step, pool_step = sem("dve_step"), sem("act_step"), sem("pool_step")
        norm_squares, norm_sum, norm_rs = sem("norm_squares"), sem("norm_sum"), sem("norm_rs")
        h_ready, h_split = sem("h_ready"), sem("h_split")
        lr_ready, lr_copied = sem("low_rank_ready"), sem("low_rank_copied")
        z_ready, ln_ready, sp_ready, sp_masked = (sem("stick_z_ready"), sem("stick_ln_ready"),
                                                  sem("stick_sp_ready"), sem("stick_sp_masked"))
        arg_ready, att_ready, att_masked, o_ready = (sem("stick_arg_ready"), sem("stick_att_ready"),
                                                     sem("stick_att_masked"), sem("stick_o_ready"))
        o_split = sem("stick_o_split")
        la_ready, la_read, soft_ready = sem("log_a_ready"), sem("log_a_read"), sem("softplus_ready")
        cum_ready, exp_ready, dec_ready = sem("cumulated"), sem("exponentials_ready"), sem("decayed_ready")
        ke_ready, sc_ready, ke_copied, sc_copied = (sem("k_end_turned"), sem("gla_scores_ready"),
                                                    sem("k_end_copied"), sem("gla_scores_copied"))
        sc_masked, ds_ready, st_ready = sem("gla_scores_masked"), sem("d_state_ready"), sem("states_ready")
        go_ready, go_copied, gs_ready = sem("gla_o_ready"), sem("gla_o_copied"), sem("gla_sums_ready")
        gr_ready = sem("gla_rs_ready")
        conv_done, mean_ready, mean_copied, centred = (sem("conv_done"), sem("conv_mean_ready"),
                                                       sem("conv_mean_copied"), sem("conv_centred"))
        cv_squared, var_ready, cv_rs, cv_scaled = (sem("conv_squared"), sem("conv_var_ready"),
                                                   sem("conv_rs_ready"), sem("conv_scaled"))
        cv_silu, gg_silu, gates_ready = sem("conv_silu_ready"), sem("gg_silu_ready"), sem("gates_ready")
        a_split, c_split, s_split = sem("conv_split"), sem("gla_split"), sem("merged_split")
        y_copied, x_updated = sem("y_copied"), sem("x_updated")
        ff_split, down_copied = sem("ffn_split"), sem("ffn_down_copied")
        stored = sem("output_stored")
        conv_taps, scans = sem("conv_taps"), sem("scans")
        htok_turned, htok_copied = sem("h_turned"), sem("h_tok_copied")
        logits_done, gap_ready, exp_done = sem("logits_done"), sem("logit_gap_ready"), sem("router_exp_done")
        routed, counted, list_ready = sem("routed"), sem("tokens_counted"), sem("overflow_list_ready")
        moe_consts = sem("moe_constants_written")
        sel_ready, sel_turned = sem("selection_ready"), sem("selection_turned")
        gathered, xe_hi_done, xe_split = sem("gathered"), sem("expert_input_high"), sem("expert_input_split")
        silu_done, act_done, turned = sem("silu_done"), sem("act_done"), sem("act_turned")
        ae_hi_done, ae_split = sem("act_high"), sem("act_split")
        ye_copied, scattered, moe_added = sem("expert_y_copied"), sem("scattered"), sem("moe_added")
        sel_zeroed, sel_w_ready = sem("selection_zeroed"), sem("weighted_selection_ready")

        block = ctx.enter_context(nc.Block())

        BANKS = {}
        uses = 0
        for u in W_UNITS:
            BANKS[u] = []
            for _ in range({"out": 2, "down": 0}.get(u[0], 1)):
                BANKS[u].append((uses % WBANKS, uses // WBANKS))
                uses += 1

        def mixer_units(layer):
            return [u for u in W_UNITS if u[1] == layer and u[0] in ("z", "out", "wo")]

        FFN_UNITS = [u for u in W_UNITS if u[0] in ("gate", "up", "down")]

        def two(ap):
            return ap.rearrange("p (a b) -> p a b", a=2)

        def wait_read(eng, u):
            for b, before in BANKS[u]:
                eng.wait_ge(bank_read[b], before + 1)

        def moe_unit(step, k, rounds=0):
            n, w = N_UNITS + k, N_W + k
            landed = step * (16 * EU // RAW) + rounds * 16 + 16 * (n // RAW + 1)
            return n % RAW, landed, k % (SPLIT + 1), step * EU + rounds * RAW + w

        def over_steps(eng, body):
            eng.wait_ge(list_ready, 1)
            n = eng.value_load(ints[0:1, 0:1], min_val=0, max_val=3)
            with eng.If(n > 0):
                with eng.Fori(0, n) as j:
                    expert = eng.value_load(ints[0:1, bass.ds(j + 1, 1)], min_val=0, max_val=N_EXP - 1)
                    body(j + N_EXP, expert)
                eng.nop()
            return n + N_EXP

        @block.sync
        def _(sp):
            def load(n, value, src):
                sp.wait_ge(released, value)
                sp.dma_start(raw[:, n % RAW, :], src).then_inc(loaded[n % RAW], 16)

            for n in range(RAW):
                sp.dma_start(raw[:, n, :], stream[n]).then_inc(loaded[n], 16)
            rounds = (N_UNITS - RAW) // RAW
            with sp.Fori(0, rounds) as r:
                for s in range(RAW):
                    load(s, r * RAW + s + 1, stream[bass.ds(r * RAW + RAW + s, 1), :, :].rearrange(
                        "a p n -> p (a n)"))
            for n in range(RAW + rounds * RAW, N_UNITS):
                load(n, n - RAW + 1, stream[n])

            def expert_step(step, expert):
                with sp.Fori(0, EU // RAW) as q:
                    for s in range(RAW):
                        load(N_UNITS + s, step * EU + q * RAW + (N_UNITS + s - RAW + 1),
                             experts[bass.ds(expert * EU + q * RAW + s, 1), :, :].rearrange(
                                 "a p n -> p (a n)"))

            with sp.Fori(0, N_EXP) as g:
                expert_step(g, g)
            over_steps(sp, expert_step)
            sp.wait_ge(x_updated, 2 * DEPTH)
            sp.dma_start(out_t, x).then_inc(stored, 16)
            sp.wait_ge(stored, 16)

        @block.gpsimd
        def _(pool):
            pool.dma_start(ar[:, C_VEC:C_VEC + N_VEC], vecs).then_inc(vec_loaded, 16)
            pool.dma_start(x, x_t).then_inc(x_loaded, 16)
            pool.memset(neg, -1.0).then_inc(consts, 1)
            pool.memset(ones, 1.0).then_inc(consts, 1)
            pool.memset(ar[:, C_EPS:C_EPS + 8], EPS).then_inc(consts, 1)
            pool.wait_ge(consts, 3)
            pool.affine_select(l_neg, neg, [[-1, P]], ALU.is_ge, 0.0, 0, 1).then_inc(consts, 1)
            pool.affine_select(ident, ones, [[-1, P]], ALU.is_equal, 0.0, 0, 1).then_inc(consts, 1)
            for layer in range(DEPTH):
                if layer:
                    pool.wait_ge(ada_reduced, 6)
                    pool.wait_ge(ff_split, PAIRS)
                pool.dma_start(wglr, glr_w[layer]).then_inc(lr_loaded, 16)
                pool.dma_start(a2_sb[0:RANK, :], a2[layer]).then_inc(lr_loaded, 16)
                pool.memset(ypad[:, :, 0:TAPS - 1], 0.0).then_inc(pad_zeroed, 1)
                for i in range(SB_HEADS + 1):
                    if i < SB_HEADS:
                        s = stick_s[i % 2][:, :, 0:P]
                        pool.wait_ge(sp_ready, layer * SB_HEADS + i + 1)
                        pool.affine_select(s, s, [[0, 2], [1, P]], ALU.is_gt, 0.0, 0, -1).then_inc(sp_masked, 1)
                    if i:
                        e = stick_e[(i - 1) % 2][:, :, 0:P]
                        pool.wait_ge(att_ready, layer * SB_HEADS + i)
                        pool.affine_select(e, e, [[0, 2], [1, P]], ALU.is_gt, 0.0, 0, -1).then_inc(att_masked, 1)
                pool.wait_ge(sc_copied, 2 * (layer + 1))
                both = area(A_GQ, 8, P)
                pool.affine_select(both, both, [[0, 8], [1, P]], ALU.is_ge, 0.0, 0, -1).then_inc(pool_step, 1)
                pool.wait_ge(pool_step, layer + 1)
                pool.memset(both[0:CH, :, CH:P], 0.0).then_inc(sc_masked, 1)
            pool.wait_ge(c_split, DEPTH)
            pool.dma_start(router_sb, router).then_inc(router_loaded, 16)
            pool.iota(iota, [[1, P]], 0, 0, allow_small_or_imprecise_dtypes=True).then_inc(moe_consts, 1)
            pool.iota(iota8, [[1, 8]], 0, 0, allow_small_or_imprecise_dtypes=True).then_inc(moe_consts, 1)
            pool.affine_select(tril, ones, [[1, P]], ALU.is_gt, 0.0, 0, -1).then_inc(moe_consts, 1)

        @block.scalar
        def _(act):
            steps, norms = [0], [0]

            def link(ins):
                steps[0] += 1
                ins.then_inc(act_step, 1)
                act.wait_ge(act_step, steps[0])

            def write_hi(u):
                slot = POS[u] % RAW
                act.wait_ge(loaded[slot], 16 * (POS[u] // RAW + 1))
                if FREED[u]:
                    act.wait_ge(consumed, FREED[u])
                act.activation(w_hi[SLOT[u]], raw[:, slot, :], ACT.Copy).then_inc(hi_written, 1)

            def rsqrt(to, tmp, sums, n, done):
                link(act.activation(tmp, sums, ACT.Ln, bias=eps, scale=1.0 / n))
                act.activation(to, tmp, ACT.Exp, scale=-0.5).then_inc(done, 1)

            def norm(src):
                norms[0] += 1
                act.activation(squares, src, ACT.Square).then_inc(norm_squares, 1)
                act.wait_ge(norm_sum, norms[0])
                rsqrt(rs, rt, M[:, 0:T], D, norm_rs)

            def copy_unit(u, to, func=ACT.Copy, scale=1.0):
                act.wait_ge(consumed, WPOS[u] + 1)
                b = BANKS[u][0][0]
                act.activation(to, two(bank[b]), func, scale=scale).then_inc(bank_read[b], 1)

            neg_b = area(C_DEC, 16)[:, 0:4]

            def evacuate(layer, i, u):
                if u[0] == "z" and i in (0, 2):
                    if i == 2:
                        wait_read(act, ("z", layer, 1, 0))
                    copy_unit(u, sig, ACT.Sigmoid)
                elif u[0] == "z" and 4 <= i < 10:
                    part, h = divmod(i - 4, 2)
                    to = sv[:, :, 256 * h:256 * h + 256] if part == 2 else (sq, sk)[part][:, 2 * h:2 * h + 2, :]
                    copy_unit(u, to, scale=SB_DH ** -0.5 if part == 0 else 1.0)
                elif u[0] == "z" and 10 <= i < Z_UNITS:
                    part, h = divmod(i - 10, 2)
                    to = gv[:, :, 256 * h:256 * h + 256] if part == 2 else \
                        (gq, gk, None, gg)[part][:, 2 * h:2 * h + 2, :]
                    copy_unit(u, to, scale=GLA_D ** -0.5 if part == 0 else 1.0)
                elif u[0] == "z" and i >= Z_UNITS:
                    j = i - Z_UNITS
                    if j == 0 and layer == 0:
                        act.wait_ge(ada_reduced, 3)
                    if j == 8:
                        act.wait_ge(la_ready, 2 * layer + 2)
                    copy_unit(u, gates[:, 2 * j:2 * j + 2, :])
                elif u[0] == "wo":
                    if i == 36:
                        act.wait_ge(s_split, layer + 1)
                    copy_unit(u, y[:, 2 * (i - 36):2 * (i - 36) + 2, :])

            def stick_ln(layer, hh):
                n = layer * SB_HEADS + hh
                e = flat(stick_e[hh % 2])
                act.wait_ge(z_ready, n + 1)
                if hh >= 2:
                    act.wait_ge(o_ready, n - 1)
                else:
                    wait_read(act, ("z", layer, 3, 0))
                link(act.activation(e, Z[hh % 2][:, 0:384], ACT.Abs))
                link(act.activation(e, e, ACT.Exp, scale=-1.0))
                act.activation(e, e, ACT.Ln, bias=1.0).then_inc(ln_ready, 1)

            def stick_att(layer, hh):
                act.wait_ge(arg_ready, layer * SB_HEADS + hh + 1)
                act.activation(flat(stick_e[hh % 2]), Z[hh % 2][:, 0:384], ACT.Exp).then_inc(att_ready, 1)

            def log_a(layer, half):
                act.wait_ge(la_ready, 2 * layer + half + 1)
                if half == 0:
                    act.wait_ge(z_ready, SB_HEADS * (layer + 1))
                for k in range(2):
                    h = 2 * half + k
                    act.activation(cum[:, h, :], M[:, T * k:T * k + T], ACT.Abs,
                                   bias=vec(layer, "gla_a_b")[:, h:h + 1]).then_inc(la_read, 1)
                    act.activation(gap[:, h, :], M[:, T * k:T * k + T], ACT.Relu,
                                   bias=neg_b[:, h:h + 1], scale=-1.0).then_inc(la_read, 1)

            def hook(layer, i):
                if i == 1:
                    if layer:
                        act.wait_ge(consumed, WPOS[FFN_UNITS[-1]] + 1)
                        for q in range(4):
                            act.activation(y[:, 2 * q:2 * q + 2, :], two(FB[q]), ACT.Copy).then_inc(down_copied, 1)
                        act.wait_ge(down_copied, 4)
                        norm(y)
                        act.wait_ge(x_updated, 2 * layer)
                    else:
                        act.wait_ge(x_loaded, 16)
                    norm(x)
                    act.activation(neg_b, vec(layer, "gla_a_b"), ACT.Copy, scale=-1.0).then_inc(lr_copied, 1)
                if i == 2:
                    act.wait_ge(lr_ready, layer + 1)
                    act.activation(glr[0:RANK, :], M[0:RANK, 0:T], ACT.Copy).then_inc(lr_copied, 1)
                if 0 <= i - 12 < SB_HEADS:
                    stick_att(layer, i - 12)
                if 0 <= i - 11 < SB_HEADS:
                    stick_ln(layer, i - 11)
                if i == 20:
                    log_a(layer, 0)
                if i == 21:
                    log_a(layer, 1)
                    act.wait_ge(la_read, 8 * (layer + 1))
                    link(act.activation(cum, cum, ACT.Exp, scale=-1.0))
                    act.activation(cum, cum, ACT.Ln, bias=1.0).then_inc(soft_ready, 1)
                if i == 22:
                    act.wait_ge(cum_ready, layer + 1)
                    act.wait_ge(o_ready, SB_HEADS * (layer + 1))
                    act.activation(e_in, cum, ACT.Exp, scale=-1.0 / 16).then_inc(exp_ready, 1)
                    act.activation(e_out, cum, ACT.Exp, scale=1.0 / 16).then_inc(exp_ready, 1)
                    act.activation(gap, gap, ACT.Exp, scale=-1.0 / 16).then_inc(exp_ready, 1)
                if i == 24:
                    act.wait_ge(dec_ready, layer + 1)
                    for t in range(2):
                        act.wait_ge(ke_ready, 2 * layer + t + 1)
                        act.activation(ket[:, 512 * t:512 * t + 512], Z[t][:, :], ACT.Copy).then_inc(ke_copied, 1)
                    for t in range(2):
                        act.wait_ge(sc_ready, 2 * layer + t + 1)
                        act.activation(s_t[:, 512 * t:512 * t + 512], O[t][:, :], ACT.Copy).then_inc(sc_copied, 1)
                if i == 26:
                    for t in range(2):
                        act.wait_ge(go_ready, 2 * layer + t + 1)
                        act.activation(gla_o[:, 2 * t:2 * t + 2, :], two(O[t]), ACT.Copy).then_inc(go_copied, 1)
                        act.activation(gla_sq[:, 2 * t:2 * t + 2, :], two(O[t]), ACT.Square).then_inc(go_copied, 1)
                if i == 27:
                    act.wait_ge(gs_ready, 2 * (layer + 1))
                    link(act.activation(gla_sq[:, 0:2, :], two(M), ACT.Ln, bias=eps, scale=1.0 / GLA_D))
                    link(act.activation(gla_sq[:, 2:4, :], two(Z[0]), ACT.Ln, bias=eps, scale=1.0 / GLA_D))
                    act.activation(gla_rs, gla_sq, ACT.Exp, scale=-0.5).then_inc(gr_ready, 1)
                    act.wait_ge(mean_ready, layer + 1)
                    act.activation(rt, Z[1][:, 0:T], ACT.Copy, scale=1.0 / CONV).then_inc(mean_copied, 1)
                if i == 28:
                    act.wait_ge(centred, layer + 1)
                    act.activation(conv_tmp, conv_acc, ACT.Square).then_inc(cv_squared, 1)
                if i == 29:
                    act.wait_ge(var_ready, layer + 1)
                    rsqrt(rs, rt, Z[1][:, 0:T], CONV, cv_rs)
                if i == 30:
                    act.activation(gg, gg, ACT.Silu).then_inc(gg_silu, 1)
                    act.wait_ge(cv_scaled, layer + 1)
                    for c in range(4):
                        act.activation(conv_tmp[:, c, :], conv_acc[:, c, :], ACT.Silu,
                                       bias=vec(layer, "conv_ln_b")[:, c:c + 1],
                                       scale=vec(layer, "conv_ln_g")[:, c:c + 1]).then_inc(cv_silu, 1)
                if i == 31:
                    for j in range(3):
                        wait_read(act, ("z", layer, Z_UNITS + G_UNITS - 1 - j, 0))
                    for b in (1, 0, 2):
                        g = gates[:, 8 * b:8 * b + 8, :]
                        act.activation(g, g, ACT.Sigmoid).then_inc(gates_ready, 1)

            def mixer_norms(layer):
                for j in range(3):
                    wait_read(act, ("wo", layer, 3 - j, 0))
                norm(y)
                act.wait_ge(x_updated, 2 * layer + 1)
                norm(x)

            act.wait_ge(vec_loaded, 16)
            act.activation(cond, ar[:, C_VEC + DEPTH * V_LAYER:C_VEC + N_VEC], ACT.Silu).then_inc(cond_ready, 1)
            act.wait_ge(consts, 5)
            for layer in range(DEPTH):
                units = mixer_units(layer)
                for i, u in enumerate(units):
                    write_hi(u)
                    if i >= LAG:
                        evacuate(layer, i - LAG, units[i - LAG])
                    hook(layer, i)
                if layer == 0:
                    for i, u in enumerate(FFN_UNITS):
                        write_hi(u)
                        if i < LAG:
                            evacuate(layer, 38 + i, units[38 + i])
                        else:
                            b = FFN_UNITS[i - LAG]
                            if b[0] == "gate":
                                if b[2] >= 2:
                                    act.wait_ge(ff_split, b[2] - 1)
                                copy_unit(b, silu_g[b[2] % 2], ACT.Silu)
                        if i == 1:
                            mixer_norms(layer)
                else:
                    for i in (38, 39):
                        evacuate(layer, i, units[i])
                    mixer_norms(layer)

            act.wait_ge(gap_ready, 1)
            act.activation(prob[:, :, 1], prob[:, :, 0], ACT.Exp).then_inc(exp_done, 1)
            for q in range(4):
                act.wait_ge(htok_turned, q + 1)
                act.activation(h_tok[:, 512 * q:512 * q + 512], (O[0], O[1], M, Z[1])[q][:, :],
                               ACT.Copy).then_inc(htok_copied, 1)

            def moe_hi(step, k, rounds=0):
                slot, landed, s, w = moe_unit(step, k, rounds)
                act.wait_ge(loaded[slot], landed)
                act.wait_ge(consumed, w - SPLIT)
                act.activation(w_hi[s], raw[:, slot, :], ACT.Copy).then_inc(hi_written, 1)

            def silu_tile(step, k, odd, rounds=0):
                act.wait_ge(consumed, moe_unit(step, k, rounds)[3] + 1)
                act.activation(silu_e[odd], bank[2 * odd][:, :], ACT.Silu).then_inc(silu_done, 1)

            def expert_step(step, expert):
                moe_hi(step, 0)
                moe_hi(step, 1)
                expert_result(step)
                moe_hi(step, 2)
                moe_hi(step, 3)
                silu_tile(step, 1, 0)
                with act.Fori(0, (FT - 1) // 2) as q:
                    for r in range(2):
                        for j in range(4):
                            moe_hi(step, 4 + 6 * r + j, q * 2)
                        silu_tile(step, 4 + 6 * r + 1, 1 - r, q * 2)
                        for j in range(4, 6):
                            moe_hi(step, 4 + 6 * r + j, q * 2)
                for k in (EU - 2, EU - 1):
                    moe_hi(step, k)

            def expert_result(step):
                act.wait_ge(sel_turned, step + 1)
                act.activation(sel_t, bank[7][:, 0:T], ACT.Copy).then_inc(ye_copied, 1)
                for half in range(2):
                    act.activation(y_e[:, 512 * half:512 * half + 512], bank[5 + half][:, :],
                                   ACT.Copy).then_inc(ye_copied, 1)

            with act.Fori(0, N_EXP) as g:
                expert_step(g, g)
            n_steps = over_steps(act, expert_step)
            expert_result(n_steps)
            norms[0] += 1
            act.wait_ge(moe_added, n_steps * 4 + 4)
            act.activation(area(A_SQ, 2048), moe_y, ACT.Square).then_inc(norm_squares, 1)
            act.wait_ge(norm_sum, norms[0])
            rsqrt(rs, rt, M[:, 0:T], D, norm_rs)

        @block.vector
        def _(dve):
            steps, norms = [0], [0]

            def link(ins):
                steps[0] += 1
                ins.then_inc(dve_step, 1)
                dve.wait_ge(dve_step, steps[0])

            def write_lo(u):
                w = WPOS[u]
                dve.wait_ge(hi_written, w + 1)
                dve.tensor_tensor(w_lo[SLOT[u]], raw[:, POS[u] % RAW, :], f32(w_hi[SLOT[u]]),
                                  ALU.subtract).then_inc(lo_written, 1)
                dve.wait_ge(lo_written, w + 1)
                dve.sem_inc(released, 1)

            def add_ada(u):
                _, layer, g, k = u
                n = POS[u]
                dve.wait_ge(loaded[n % RAW], 16 * (n // RAW + 1))
                acc = ada_acc[layer, g]
                w = raw[:, n % RAW, :]
                if k == 0:
                    if (layer, g) == (0, 1):
                        dve.wait_ge(ada_reduced, 1)
                    ins = dve.tensor_scalar(acc, w, cond[:, 0:1], None, ALU.mult)
                else:
                    ins = dve.scalar_tensor_tensor(acc, w, cond[:, k:k + 1], acc, ALU.mult, ALU.add)
                ins.then_inc(released, 1)
                dve.wait_ge(released, n + 1)
                if k == KC - 1:
                    dve.sem_inc(ada_summed, 1)

            def finish_mods(layer, g):
                dve.wait_ge(ada_reduced, 3 * layer + g + 1)
                at = C_MOD + 80 * layer + 16 * g
                link(dve.tensor_tensor(ar[:, at:at + 16], M[:, 16 * g:16 * g + 16],
                                       vec(layer, "ada_b")[:, 16 * g:16 * g + 16], ALU.add))
                if g == 0:
                    ins = dve.scalar_tensor_tensor(mod(layer, A_M), mod(layer, SC_M), 1.0,
                                                   vec(layer, "mix_pre_g"), ALU.add, ALU.mult)
                elif g == 1:
                    ins = dve.tensor_tensor(mod(layer, P_M), mod(layer, G_M), vec(layer, "mix_post_g"), ALU.mult)
                else:
                    link(dve.tensor_tensor(mod(layer, P_F), mod(layer, G_F), vec(layer, "ffn_post_g"), ALU.mult))
                    ins = dve.scalar_tensor_tensor(mod(layer, A_F), mod(layer, SC_F), 1.0,
                                                   vec(layer, "ffn_pre_g"), ALU.add, ALU.mult)
                ins.then_inc(mods_ready, 1)
                dve.wait_ge(mods_ready, 3 * layer + g + 1)

            def split(hi, lo, src, done, value):
                link(dve.tensor_copy(hi, src))
                dve.tensor_tensor(lo, src, f32(hi), ALU.subtract).then_inc(done, 1)
                dve.wait_ge(done, value)

            def norm_in(layer, a, b, split_too=True):
                norms[0] += 1
                dve.wait_ge(norm_rs, norms[0])
                link(dve.tensor_tensor(hf, x, bcast(rs, KC), ALU.mult))
                for c in range(KC):
                    ins = dve.tensor_scalar(hf[:, c, :], hf[:, c, :], mod(layer, a)[:, c:c + 1],
                                            mod(layer, b)[:, c:c + 1], ALU.mult, ALU.add)
                    ins.then_inc(h_ready, 1)
                count = (2 * layer + (a == A_F) + 1)
                dve.wait_ge(h_ready, KC * count)
                if split_too:
                    split(h_hi, h_lo, hf, h_split, count)

            def norm_out(src, layer, p, value):
                norms[0] += 1
                dve.wait_ge(norm_rs, norms[0])
                link(dve.tensor_tensor(src, src, bcast(rs, KC), ALU.mult))
                for c in range(KC):
                    ins = dve.scalar_tensor_tensor(x[:, c, :], src[:, c, :], mod(layer, p)[:, c:c + 1],
                                                   x[:, c, :], ALU.mult, ALU.add)
                    if c < KC - 1:
                        link(ins)
                ins.then_inc(x_updated, 1)
                dve.wait_ge(x_updated, value)

            def glu(layer, h):
                u = ("z", layer, 2 * h + 1, 0)
                wait_read(dve, ("z", layer, 2 * h, 0))
                dve.wait_ge(consumed, WPOS[u] + 1)
                dve.wait_ge(pad_zeroed, layer + 1)
                b, before = BANKS[u][0]
                dve.tensor_tensor(ypad[:, 2 * h:2 * h + 2, TAPS - 1:YW], two(bank[b]), sig,
                                  ALU.mult).then_inc(bank_read[b], 1)
                dve.wait_ge(bank_read[b], before + 1)

            taps_done = {}

            def taps(layer, pair, k0, k1):
                for k in range(k0, min(k1, TAPS)):
                    for c in (2 * pair, 2 * pair + 1):
                        w = vec(layer, "conv_dw")[:, TAPS * c + k:TAPS * c + k + 1]
                        src, acc = ypad[:, c, k:k + T], conv_acc[:, c, :]
                        if k == 0:
                            ins = dve.tensor_scalar(acc, src, w, vec(layer, "conv_dw_b")[:, c:c + 1],
                                                    ALU.mult, ALU.add)
                        else:
                            dve.wait_ge(conv_taps, taps_done[c])
                            ins = dve.scalar_tensor_tensor(acc, src, w, acc, ALU.mult, ALU.add)
                        ins.then_inc(conv_taps, 1)
                        tap_count[0] += 1
                        taps_done[c] = tap_count[0]

            tap_count = [0]

            def stick_sp(layer, hh):
                n = layer * SB_HEADS + hh
                dve.wait_ge(ln_ready, n + 1)
                if hh >= 2:
                    dve.wait_ge(arg_ready, n - 1)
                dve.scalar_tensor_tensor(flat(stick_s[hh % 2]), Z[hh % 2][:, 0:384], 0.0,
                                         flat(stick_e[hh % 2]), ALU.max, ALU.add).then_inc(sp_ready, 1)

            def stick_out(layer, c):
                dve.wait_ge(o_ready, layer * SB_HEADS + 2 * c + 2)
                split(br_hi[1][:, c, :], br_lo[1][:, c, :], O[c % 2][:, 0:T], o_split, 4 * layer + c + 1)

            def gla_cum(layer):
                dve.wait_ge(soft_ready, layer + 1)
                link(dve.tensor_tensor(cum, cum, gap, ALU.add))
                for h in range(GLA_HEADS):
                    for c in range(4):
                        s = cum[:, h, CH * c:CH * c + CH]
                        ins = dve.tensor_tensor_scan(gap[:, h, CH * c:CH * c + CH], ones[:, 0:CH], s, 0.0,
                                                     ALU.mult, ALU.add)
                        ins.then_inc(scans, 1)
                dve.wait_ge(scans, 16 * (layer + 1))
                link(dve.tensor_copy(cum, gap))
                c4 = area(A_SQ, 16, CH)
                dve.tensor_tensor(area(A_SK, 16, CH), c4[:, :, CH - 1:CH].to_broadcast([P, 16, CH]), c4,
                                  ALU.subtract).then_inc(cum_ready, 1)

            def gla_decay(layer):
                dve.wait_ge(exp_ready, 3 * (layer + 1))
                link(dve.tensor_copy(area(C_DEC, 16), area(A_SV, 16, CH)[:, :, CH - 1]))
                link(dve.tensor_tensor(e_in, gq, e_in, ALU.mult))
                link(dve.tensor_tensor(gap, gk, gap, ALU.mult))
                dve.tensor_tensor(e_out, gk, e_out, ALU.mult).then_inc(dec_ready, 1)

            def gla_states(layer):
                for j in range(3):
                    src = (M, Z[0], Z[1])[j]
                    dve.wait_ge(ds_ready, 3 * layer + j + 1)
                    if j == 0:
                        ins = dve.tensor_copy(states[0], src[:, :])
                        link(ins)
                    else:
                        for h in range(GLA_HEADS):
                            c = P * h
                            ins = dve.scalar_tensor_tensor(states[j][:, c:c + P], states[j - 1][:, c:c + P],
                                                           decay[:, h, j:j + 1], src[:, c:c + P],
                                                           ALU.mult, ALU.add)
                            link(ins)
                dve.sem_inc(st_ready, 1)

            def gla_scale(layer):
                dve.wait_ge(gr_ready, layer + 1)
                for h in range(GLA_HEADS):
                    link(dve.scalar_tensor_tensor(gla_o[:, h, :], gla_o[:, h, :],
                                                  vec(layer, "gla_norm_g")[:, h:h + 1], gla_rs[:, h, :],
                                                  ALU.mult, ALU.mult))

            def merge(layer, i, u):
                _, _, b, half = u
                dve.wait_ge(consumed, WPOS[u] + 1)
                if half == 0:
                    dve.wait_ge(gates_ready, 3 * layer + 1 + (1, 0, 2).index(b))
                if i == 30:
                    dve.wait_ge(cv_silu, 4 * (layer + 1))
                for j in range(2):
                    q = 2 * half + j
                    bk, before = BANKS[u][j]
                    g = gates[:, 8 * b + 2 * q:8 * b + 2 * q + 2, :]
                    to = merged[:, 2 * q:2 * q + 2, :] if b == 1 else g
                    dve.tensor_tensor(to, two(bank[bk]), g, ALU.mult).then_inc(bank_read[bk], 1)
                    dve.wait_ge(bank_read[bk], before + 1)
                    if b != 1:
                        link(dve.tensor_tensor(merged[:, 2 * q:2 * q + 2, :], merged[:, 2 * q:2 * q + 2, :],
                                               g, ALU.add))

            def hook(layer, i):
                if i == 1:
                    if layer == 0:
                        finish_mods(0, 0)
                    else:
                        norm_out(y, 0, P_F, 2 * layer)
                    norm_in(layer, A_M, SH_M)
                if layer == 0 and i == 12:
                    finish_mods(0, 1)
                if layer == 0 and i == 19:
                    finish_mods(0, 2)
                if 0 <= i - 11 < SB_HEADS:
                    stick_sp(layer, i - 11)
                if i >= 14 and (i - 14) % 2 == 0 and (i - 14) // 2 < 4:
                    stick_out(layer, (i - 14) // 2)
                if i == 3:
                    glu(layer, 0)
                if i == 5:
                    glu(layer, 1)
                if 4 <= i < 15:
                    taps(layer, 0, 3 * (i - 4), 3 * (i - 4) + 3)
                if 15 <= i < 26:
                    taps(layer, 1, 3 * (i - 15), 3 * (i - 15) + 3)
                if i == 26:
                    dve.wait_ge(conv_taps, tap_count[0])
                    dve.sem_inc(conv_done, 1)
                if i == 21:
                    gla_cum(layer)
                if i == 22:
                    gla_decay(layer)
                if i == 25:
                    gla_states(layer)
                if i == 27:
                    gla_scale(layer)
                    dve.wait_ge(mean_copied, layer + 1)
                    dve.tensor_tensor(conv_acc, conv_acc, bcast(rt, 4), ALU.subtract).then_inc(centred, 1)
                if i == 29:
                    dve.wait_ge(centred, layer + 1)
                    dve.wait_ge(cv_rs, layer + 1)
                    dve.tensor_tensor(conv_acc, conv_acc, bcast(rs, 4), ALU.mult).then_inc(cv_scaled, 1)
                if i == 30:
                    dve.wait_ge(cv_silu, 4 * (layer + 1))
                    split(br_hi[0], br_lo[0], conv_tmp, a_split, layer + 1)
                if i == 31:
                    dve.wait_ge(gg_silu, layer + 1)
                    link(dve.tensor_tensor(gla_o, gla_o, gg, ALU.mult))
                    split(br_hi[2], br_lo[2], gla_o, c_split, layer + 1)
                if i == 37:
                    split(h_hi, h_lo, merged, s_split, layer + 1)

            def mixer_norms(layer):
                norm_out(y, layer, P_M, 2 * layer + 1)
                norm_in(layer, A_F, SH_F, split_too=(layer == 0))

            dve.wait_ge(cond_ready, 1)
            order = iter(PLAN)

            def take(u):
                for v in order:
                    if v == u:
                        write_lo(u)
                        return
                    add_ada(v)

            for layer in range(DEPTH):
                units = mixer_units(layer)
                for i, u in enumerate(units):
                    take(u)
                    if i >= LAG and units[i - LAG][0] == "out":
                        merge(layer, i - LAG, units[i - LAG])
                    hook(layer, i)
                if layer == 0:
                    for i, u in enumerate(FFN_UNITS):
                        take(u)
                        if i == 1:
                            mixer_norms(layer)
                        if i >= LAG and FFN_UNITS[i - LAG][0] == "up":
                            b = FFN_UNITS[i - LAG]
                            t = b[2]
                            wait_read(dve, ("gate", 0, t, 0))
                            dve.wait_ge(consumed, WPOS[b] + 1)
                            bk, before = BANKS[b][0]
                            dve.tensor_tensor(prod[t % 2], two(bank[bk]), silu_g[t % 2],
                                              ALU.mult).then_inc(bank_read[bk], 1)
                            dve.wait_ge(bank_read[bk], before + 1)
                            split(ff_hi[t % 2], ff_lo[t % 2], prod[t % 2], ff_split, t + 1)
                        for g, t in enumerate(ADA_TURN):
                            if u == ("up", 0, t, 0):
                                finish_mods(1, g)
                else:
                    mixer_norms(layer)

            dve.wait_ge(moe_consts, 3)
            dve.wait_ge(logits_done, 1)
            link(dve.tensor_copy(logits, Z[0][:, 0:16]))
            for t in range(2):
                lg = logits[:, 8 * t:8 * t + 8]
                link(dve.max(top[:, t, :], lg))
                link(dve.max_index(index[:, t, :], top[:, t, :], lg))
                link(dve.tensor_copy(index_f[:, t, :], index[:, t, :]))
                link(dve.tensor_tensor(prob[:, t, 0:1], top[:, t, 1:2], top[:, t, 0:1], ALU.subtract))
            dve.sem_inc(gap_ready, 1)
            dve.wait_ge(exp_done, 1)
            link(dve.tensor_scalar(prob[:, :, 0], prob[:, :, 1], 1.0, None, ALU.add))
            link(dve.reciprocal(prob[:, :, 0], prob[:, :, 0]))
            link(dve.tensor_tensor(prob[:, :, 1], prob[:, :, 1], prob[:, :, 0], ALU.mult))
            for t in range(2):
                link(dve.tensor_scalar(pick[:, t, :], iota8, index_f[:, t, 0:1], None, ALU.is_equal))
                link(dve.tensor_scalar(pick2[:, t, :], iota8, index_f[:, t, 1:2], None, ALU.is_equal))
                link(dve.tensor_scalar(comb[:, t, :], pick[:, t, :], prob[:, t, 0:1], None, ALU.mult))
                link(dve.scalar_tensor_tensor(comb[:, t, :], pick2[:, t, :], prob[:, t, 1:2],
                                              comb[:, t, :], ALU.mult, ALU.add))
                link(dve.tensor_tensor(pick[:, t, :], pick[:, t, :], pick2[:, t, :], ALU.add))
            dve.sem_inc(routed, 1)
            dve.wait_ge(counted, 1)
            for t in range(2):
                r = Z[0][:, 16 + 8 * t:24 + 8 * t]
                link(dve.tensor_copy(places[:, t, 0:8], r))
                link(dve.tensor_scalar(places[:, t, 8:16], r, float(P), None, ALU.subtract))
                for i in range(2):
                    link(dve.tensor_copy(chosen[:, t, 8 * i:8 * i + 8], pick[:, t, :]))
                    link(dve.tensor_copy(weights[:, t, 8 * i:8 * i + 8], comb[:, t, :]))
            link(dve.tensor_scalar(over, Z[0][:, 32:40], float(P), None, ALU.is_gt))
            link(dve.tensor_tensor_scan(place8, ones[:, 0:8], over, 0.0, ALU.mult, ALU.add))
            link(dve.tensor_copy(list_f[:, 0:1], place8[:, 7:8]))
            for j in range(3):
                link(dve.scalar_tensor_tensor(hits, place8, float(j + 1), over, ALU.is_equal, ALU.mult))
                link(dve.tensor_tensor(hits, hits, iota8, ALU.mult))
                link(dve.reduce_sum(list_f[:, j + 1:j + 2], hits, mybir.AxisListType.X))
            link(dve.tensor_copy(ints[:, 0:4], list_f[:, 0:4]))
            link(dve.tensor_copy(column_f[:, 0:8], iota8))
            link(dve.memset(column_f[:, 8:12], 0.0))
            link(dve.tensor_scalar(column_f[:, 8:11], list_f[:, 1:4], float(N_EXP), None, ALU.add))
            link(dve.tensor_copy(ints[:, 8:20], column_f))
            dve.sem_inc(list_ready, 1)
            link(dve.memset(moe_y, 0.0))
            dve.memset(sel_w, 0.0).then_inc(sel_zeroed, 1)

            def moe_lo(step, k, rounds=0):
                slot, _, s, w = moe_unit(step, k, rounds)
                dve.wait_ge(hi_written, w + 1)
                dve.tensor_tensor(w_lo[s], raw[:, slot, :], f32(w_hi[s]),
                                  ALU.subtract).then_inc(lo_written, 1)
                dve.wait_ge(lo_written, w + 1)
                dve.sem_inc(released, 1)

            def multiply(step, k, odd, t, rounds=0):
                dve.wait_ge(silu_done, step * FT + t + 1)
                dve.wait_ge(consumed, moe_unit(step, k, rounds)[3] + 1)
                dve.tensor_tensor(act_e[odd], bank[2 * odd + 1][:, :], silu_e[odd],
                                  ALU.mult).then_inc(act_done, 1)

            def split_tile(step, odd, t):
                dve.wait_ge(turned, step * FT + t + 1)
                dve.tensor_copy(ae_hi[odd], bank[4][:, :]).then_inc(ae_hi_done, 1)
                dve.wait_ge(ae_hi_done, step * FT + t + 1)
                dve.tensor_tensor(ae_lo[odd], bank[4][:, :], f32(ae_hi[odd]), ALU.subtract).then_inc(ae_split, 1)

            def select(step, to, w, ready):
                column = dve.value_load(ints[0:1, bass.ds(step + 8, 1)], min_val=0, max_val=15)
                for t in range(2):
                    col = bass.ds(column + 16 * t, 1)
                    dve.tensor_scalar(to[:, P * t:P * t + P], iota, places_f[:, col], w[:, col],
                                      ALU.is_equal, ALU.mult).then_inc(ready, 1)

            def split_input(step, half):
                dve.wait_ge(gathered, step * 2 + half + 1)
                src = (bank[7], bank[4])[half]
                c = 512 * half
                dve.tensor_copy(xe_hi[:, c:c + 512], src[:, :]).then_inc(xe_hi_done, 1)
                dve.wait_ge(xe_hi_done, step * 2 + half + 1)
                dve.tensor_tensor(xe_lo[:, c:c + 512], src[:, :], f32(xe_hi[:, c:c + 512]),
                                  ALU.subtract).then_inc(xe_split, 1)

            def add_result(step):
                for p in range(4):
                    dve.wait_ge(scattered, step * 4 + p + 1)
                    to = moe_y[:, 512 * p:512 * p + 512]
                    dve.tensor_tensor(to, to, SCATTER[p][:, :], ALU.add).then_inc(moe_added, 1)

            def expert_step(step, expert):
                for k in range(4):
                    moe_lo(step, k)
                add_result(step)
                dve.wait_ge(sel_turned, step + 1)
                select(step, sel_w, weights_f, sel_w_ready)
                multiply(step, 3, 0, 0)
                with dve.Fori(0, (FT - 1) // 2) as q:
                    for r in range(2):
                        t = q * 2 + (1 + r)
                        moe_lo(step, 4 + 6 * r, q * 2)
                        split_tile(step, r, t - 1)
                        for j in range(1, 6):
                            moe_lo(step, 4 + 6 * r + j, q * 2)
                        multiply(step, 4 + 6 * r + 3, 1 - r, t, q * 2)
                select(step + 1, sel, chosen_f, sel_ready)
                split_tile(step, 0, FT - 1)
                for half in range(2):
                    moe_lo(step, EU - 2 + half)
                    split_input(step + 1, half)

            select(0, sel, chosen_f, sel_ready)
            for half in range(2):
                split_input(0, half)
            with dve.Fori(0, N_EXP) as g:
                expert_step(g, g)
            add_result(over_steps(dve, expert_step))
            norm_out(area(A_GATES + 2048, KC, T), 1, P_F, 2 * DEPTH)

        @block.tensor
        def _(pe):
            norms = [0]
            pe.wait_ge(consts, 5)

            def parts(w, slot):
                return ((w_hi[slot], True), (w_hi[slot], False), (w_lo[slot], True))

            def reduce_mods(layer, g):
                pe.wait_ge(ada_summed, 3 * layer + g + 1)
                acc = ada_acc[layer, g]
                for c in range(16):
                    mm = pe.matmul(M[:, 16 * g + c:16 * g + c + 1], acc[:, P * c:P * c + P], ones[:, 0:1],
                                   start=True, stop=True)
                mm.then_inc(ada_reduced, 1)

            def norm_sums():
                norms[0] += 1
                pe.wait_ge(norm_squares, norms[0])
                for c in range(KC):
                    mm = pe.matmul(M[:, 0:T], ones, squares[:, c, :], start=(c == 0), stop=(c == KC - 1))
                mm.then_inc(norm_sum, 1)

            def begin(u):
                pe.wait_ge(lo_written, WPOS[u] + 1)
                for b, before in BANKS[u]:
                    if before:
                        pe.wait_ge(bank_read[b], before)
                return SLOT[u]

            def project(u, hi, lo):
                s = begin(u)
                out = two(bank[BANKS[u][0][0]])
                for c in range(2):
                    for k in range(KC):
                        for n, (w, high) in enumerate(parts(u, s)):
                            mm = pe.matmul(out[:, c, :], w[:, 256 * k + P * c:256 * k + P * c + P],
                                           (hi if high else lo)[:, k, :],
                                           start=(k == 0 and n == 0), stop=(k == KC - 1 and n == 2))
                mm.then_inc(consumed, 1)

            def project_tokens(u, hi, lo):
                s = begin(u)
                out = two(bank[BANKS[u][0][0]])
                for t in range(2):
                    for k in range(KC):
                        for n, (w, high) in enumerate(parts(u, s)):
                            mm = pe.matmul(out[:, t, :], (hi if high else lo)[:, k, P * t:P * t + P],
                                           w[:, 256 * k:256 * k + 256],
                                           start=(k == 0 and n == 0), stop=(k == KC - 1 and n == 2))
                mm.then_inc(consumed, 1)

            def project_branch(u, hi, lo):
                s = begin(u)
                for c in range(4):
                    out = two(bank[BANKS[u][c // 2][0]])
                    for k in range(4):
                        for n, (w, high) in enumerate(parts(u, s)):
                            mm = pe.matmul(out[:, c % 2, :], w[:, 512 * k + P * c:512 * k + P * c + P],
                                           (hi if high else lo)[:, k, :],
                                           start=(k == 0 and n == 0), stop=(k == 3 and n == 2))
                mm.then_inc(consumed, 1)

            def project_down(u):
                t = u[2]
                pe.wait_ge(ff_split, t + 1)
                s = begin(u)
                for f in range(2):
                    for c in range(KC):
                        out = two(FB[c // 2])
                        for n, (w, high) in enumerate(parts(u, s)):
                            first = t == 0 and f == 0 and n == 0 and c % 2 == 0
                            last = t == PAIRS - 1 and f == 1 and n == 2
                            mm = pe.matmul(out[:, c % 2, :], w[:, 1024 * f + P * c:1024 * f + P * c + P],
                                           (ff_hi if high else ff_lo)[t % 2][:, f, :],
                                           start=first, stop=last, skip_group_check=True)
                mm.then_inc(consumed, 1)

            def stick_z(layer, hh):
                n, c, p = layer * SB_HEADS + hh, hh // 2, 64 * (hh % 2)
                if hh >= 2:
                    pe.wait_ge(att_ready, n - 1)
                q, k = sq[p:p + 64, c, :], sk[p:p + 64, c, :]
                pe.matmul(Z[hh % 2][:, 0:T], k[:, 0:P], q, start=True, stop=False, skip_group_check=True)
                pe.matmul(Z[hh % 2][:, T:T + P], k[:, P:T], q[:, P:T], start=False, stop=False,
                          skip_group_check=True).then_inc(z_ready, 1)

            def stick_sum(layer, hh):
                z, s = Z[hh % 2], flat(stick_s[hh % 2])
                pe.wait_ge(sp_masked, layer * SB_HEADS + hh + 1)
                pe.matmul(z[:, 0:T], l_neg, s[:, 0:T], start=False, stop=False, skip_group_check=True)
                pe.matmul(z[:, P:T], neg, s[:, T:T + P], start=False, stop=False, skip_group_check=True)
                pe.matmul(z[:, T:T + P], l_neg, s[:, T:T + P], start=False, stop=True,
                          skip_group_check=True).then_inc(arg_ready, 1)

            def stick_o(layer, hh):
                n, c, p = layer * SB_HEADS + hh, hh // 2, 64 * (hh % 2)
                if c >= 2 and hh % 2 == 0:
                    pe.wait_ge(o_split, 4 * layer + c - 1)
                pe.wait_ge(att_masked, n + 1)
                e = flat(stick_e[hh % 2])
                out = O[c % 2][p:p + 64, :]
                pe.matmul(out[:, 0:T], sv[:, 0, 64 * hh:64 * hh + 64], e[:, 0:T], start=True, stop=False,
                          skip_group_check=True)
                pe.matmul(out[:, P:T], sv[:, 1, 64 * hh:64 * hh + 64], e[:, T:T + P], start=False, stop=True,
                          skip_group_check=True).then_inc(o_ready, 1)

            def low_rank(layer):
                pe.wait_ge(lr_loaded, 32 * (layer + 1))
                pe.wait_ge(norm_rs, norms[0])
                for k in range(KC):
                    mm = pe.matmul(M[0:RANK, 0:T], wglr[:, k, :], hf[:, k, :], start=(k == 0),
                                   stop=(k == KC - 1))
                mm.then_inc(lr_ready, 1)

            def log_a(layer, half):
                if half:
                    pe.wait_ge(la_read, 8 * layer + 4)
                else:
                    pe.wait_ge(lr_copied, 2 * (layer + 1))
                    pe.wait_ge(mods_ready, 3)
                for k in range(2):
                    h = 2 * half + k
                    mm = pe.matmul(M[:, T * k:T * k + T], a2_sb[0:RANK, P * h:P * h + P], glr[0:RANK, :],
                                   start=True, stop=True)
                mm.then_inc(la_ready, 1)

            def gla_turn(layer):
                pe.wait_ge(dec_ready, layer + 1)
                pe.wait_ge(o_split, 4 * (layer + 1))
                for t in range(2):
                    for h in range(GLA_HEADS):
                        mm = pe.transpose(Z[t][:, P * h:P * h + P], gap[:, h, P * t:P * t + P], ident)
                    mm.then_inc(ke_ready, 1)
                for t in range(2):
                    for h in range(GLA_HEADS):
                        mm = pe.matmul(O[t][:, P * h:P * h + P], e_out[:, h, P * t:P * t + P],
                                       e_in[:, h, P * t:P * t + P], start=True, stop=True)
                    mm.then_inc(sc_ready, 1)

            def gla_states(layer):
                pe.wait_ge(ke_copied, 2 * (layer + 1))
                pe.wait_ge(la_read, 8 * (layer + 1))
                for j in range(3):
                    p, t = CH * (j % 2), j // 2
                    for h in range(GLA_HEADS):
                        mm = pe.matmul((M, Z[0], Z[1])[j][:, P * h:P * h + P],
                                       ket[p:p + CH, 512 * t + P * h:512 * t + P * h + P],
                                       gv[p:p + CH, t, P * h:P * h + P], start=True, stop=True)
                    mm.then_inc(ds_ready, 1)

            def gla_out(layer):
                pe.wait_ge(st_ready, layer + 1)
                pe.wait_ge(sc_masked, layer + 1)
                for h in range(GLA_HEADS):
                    out = two(O[h // 2])[:, h % 2, :]
                    for t in range(2):
                        pe.matmul(out[:, P * t:P * t + P], gv[:, t, P * h:P * h + P],
                                  s_t[:, 512 * t + P * h:512 * t + P * h + P], start=(t == 0), stop=False,
                                  skip_group_check=True)
                    for j in range(1, 4):
                        mm = pe.matmul(out[:, CH * j:CH * j + CH], states[j - 1][:, P * h:P * h + P],
                                       e_in[:, h, CH * j:CH * j + CH], start=False, stop=(j == 3),
                                       skip_group_check=True)
                    if h % 2:
                        mm.then_inc(go_ready, 1)

            def gla_sums(layer):
                pe.wait_ge(go_copied, 4 * (layer + 1))
                for t in range(2):
                    pe.matmul((M, Z[0])[t][:, :], ones, area(A_ST + 512 * t, 512), start=True,
                              stop=True).then_inc(gs_ready, 1)

            def conv_sums(layer, src, ready, value, done):
                pe.wait_ge(ready, value)
                for c in range(4):
                    mm = pe.matmul(Z[1][:, 0:T], ones, src[:, c, :], start=(c == 0), stop=(c == 3))
                mm.then_inc(done, 1)

            def hook(layer, i):
                if i == 0:
                    low_rank(layer)
                if layer == 0 and i == 10:
                    pe.wait_ge(lr_copied, 2)
                    reduce_mods(0, 1)
                if layer == 0 and i == 17:
                    pe.wait_ge(mods_ready, 2)
                    reduce_mods(0, 2)
                if 0 <= i - 12 < SB_HEADS:
                    stick_o(layer, i - 12)
                if 0 <= i - 11 < SB_HEADS:
                    stick_sum(layer, i - 11)
                if 0 <= i - 10 < SB_HEADS:
                    if i == 10:
                        wait_read(pe, ("z", layer, 7, 0))
                    if i == 12:
                        wait_read(pe, ("z", layer, 9, 0))
                    stick_z(layer, i - 10)
                if i == 19:
                    log_a(layer, 0)
                if i == 20:
                    log_a(layer, 1)
                if i == 23:
                    gla_turn(layer)
                if i == 24:
                    gla_states(layer)
                if i == 25:
                    gla_out(layer)
                if i == 26:
                    gla_sums(layer)
                    conv_sums(layer, conv_acc, conv_done, layer + 1, mean_ready)
                if i == 28:
                    conv_sums(layer, conv_tmp, cv_squared, layer + 1, var_ready)

            reduce_mods(0, 0)
            for layer in range(DEPTH):
                if layer == 0:
                    pe.wait_ge(mods_ready, 1)
                else:
                    pe.wait_ge(mods_ready, 6)
                    norm_sums()
                norm_sums()
                for i, u in enumerate(mixer_units(layer)):
                    if i == 0:
                        pe.wait_ge(h_split, 2 * layer + 1)
                    if u[0] == "z":
                        (project_tokens if z_columns()[u[2]][1] else project)(u, h_hi, h_lo)
                    elif u[0] == "out":
                        b = u[2]
                        if b == 0:
                            pe.wait_ge(a_split, layer + 1)
                        if b == 2:
                            pe.wait_ge(c_split, layer + 1)
                        project_branch(u, br_hi[b], br_lo[b])
                    else:
                        if u[2] == 0:
                            pe.wait_ge(s_split, layer + 1)
                        project(u, h_hi, h_lo)
                    hook(layer, i)
                norm_sums()
                norm_sums()
                if layer == 0:
                    pe.wait_ge(h_split, 2)
                    for u in FFN_UNITS:
                        if u[0] == "down":
                            project_down(u)
                        else:
                            project(u, h_hi, h_lo)
                        for g, t in enumerate(ADA_TURN):
                            if u == ("gate", 0, t, 0):
                                if g:
                                    pe.wait_ge(mods_ready, 3 + g)
                                reduce_mods(1, g)

            pe.wait_ge(router_loaded, 16)
            pe.wait_ge(h_ready, 4 * KC)
            for t in range(2):
                for k in range(KC):
                    mm = pe.matmul(Z[0][:, 8 * t:8 * t + 8], hf[:, k, P * t:P * t + P], router_sb[:, k, :],
                                   start=(k == 0), stop=(k == KC - 1))
            mm.then_inc(logits_done, 1)
            for q in range(4):
                t, half = divmod(q, 2)
                for c in range(4):
                    mm = pe.transpose((O[0], O[1], M, Z[1])[q][:, P * c:P * c + P],
                                      hf[:, 4 * half + c, P * t:P * t + P], ident)
                mm.then_inc(htok_turned, 1)
            pe.wait_ge(routed, 1)
            pe.matmul(Z[0][:, 16:24], tril, pick_f[:, 0:8], start=True, stop=True)
            pe.matmul(Z[0][:, 24:32], ones, pick_f[:, 0:8], start=True, stop=False)
            pe.matmul(Z[0][:, 24:32], tril, pick_f[:, 8:16], start=False, stop=True)
            pe.matmul(Z[0][:, 32:40], ones, pick_f[:, 0:8], start=True, stop=False)
            pe.matmul(Z[0][:, 32:40], ones, pick_f[:, 8:16], start=False, stop=True).then_inc(counted, 1)
            pe.wait_ge(htok_copied, 4)
            pe.wait_ge(sel_zeroed, 1)

            def moe_begin(step, k, rounds=0):
                _, _, s, w = moe_unit(step, k, rounds)
                pe.wait_ge(lo_written, w + 1)
                return s

            def gate_up(step, k, b, half, rounds=0):
                s = moe_begin(step, k, rounds)
                for kk in range(4):
                    c = P * (4 * half + kk)
                    for n, (w, high) in enumerate(parts(None, s)):
                        mm = pe.matmul(bank[b][:, :], (xe_hi if high else xe_lo)[:, c:c + P],
                                       w[:, 512 * kk:512 * kk + 512],
                                       start=(half == 0 and kk == 0 and n == 0),
                                       stop=(half == 1 and kk == 3 and n == 2))
                mm.then_inc(consumed, 1)

            def down(step, k, odd, half, t, first=False, last=False, rounds=0):
                if half == 0:
                    pe.wait_ge(ae_split, step * FT + t + 1)
                s = moe_begin(step, k, rounds)
                for f in range(2):
                    c = P * (2 * half + f)
                    for d in range(2):
                        for n, (w, high) in enumerate(parts(None, s)):
                            mm = pe.matmul(bank[5 + d][:, :], (ae_hi if high else ae_lo)[odd][:, c:c + P],
                                           w[:, 1024 * f + 512 * d:1024 * f + 512 * d + 512],
                                           start=(first and half == 0 and f == 0 and n == 0),
                                           stop=(last and half == 1 and f == 1 and n == 2),
                                           skip_group_check=True)
                mm.then_inc(consumed, 1)

            def turn(step, odd, t):
                pe.wait_ge(act_done, step * FT + t + 1)
                for c in range(4):
                    mm = pe.transpose(bank[4][:, P * c:P * c + P], act_e[odd][:, P * c:P * c + P], ident)
                mm.then_inc(turned, 1)

            def gather(step, half):
                if half == 0:
                    pe.wait_ge(sel_ready, step * 2 + 2)
                for c in range(4):
                    for t in range(2):
                        at = D * t + P * (4 * half + c)
                        mm = pe.matmul((bank[7], bank[4])[half][:, P * c:P * c + P],
                                       h_tok[:, at:at + P], sel[:, P * t:P * t + P],
                                       start=(t == 0), stop=(t == 1))
                mm.then_inc(gathered, 1)

            def turn_selection():
                for t in range(2):
                    mm = pe.transpose(bank[7][:, P * t:P * t + P], sel_w[:, P * t:P * t + P], ident)
                mm.then_inc(sel_turned, 1)

            def scatter(step):
                pe.wait_ge(ye_copied, step * 3 + 3)
                pe.wait_ge(xe_split, step * 2 + 2)
                for p in range(4):
                    for c in range(2):
                        d = P * (2 * p + c)
                        mm = pe.matmul(SCATTER[p][:, T * c:T * c + T], y_e[:, d:d + P], sel_t,
                                       start=True, stop=True)
                    mm.then_inc(scattered, 1)

            def expert_step(step, expert):
                pe.wait_ge(xe_split, step * 2 + 2)
                for k in range(2):
                    gate_up(step, k, 0, k)
                scatter(step)
                for k in range(2):
                    gate_up(step, 2 + k, 1, k)
                pe.wait_ge(moe_added, step * 4 + 4)
                turn(step, 0, 0)
                for r in range(2):
                    tile(step, r, 0, r + 1, r == 0)
                with pe.Fori(1, (FT - 1) // 2) as q:
                    for r in range(2):
                        tile(step, r, q * 2, q * 2 + (1 + r), False)
                gather(step + 1, 0)
                pe.wait_ge(ae_split, step * FT + FT)
                gather(step + 1, 1)
                for half in range(2):
                    down(step, EU - 2 + half, 0, half, FT - 1, last=True)
                pe.wait_ge(xe_split, step * 2 + 3)
                pe.wait_ge(sel_w_ready, step * 2 + 2)
                turn_selection()

            def tile(step, r, rounds, t, first):
                k, odd = 4 + 6 * r, 1 - r
                for j in range(2):
                    gate_up(step, k + j, 2 * odd, j, rounds)
                for j in range(2):
                    gate_up(step, k + 2 + j, 2 * odd + 1, j, rounds)
                down(step, k + 4, 1 - odd, 0, t - 1, first=first, rounds=rounds)
                turn(step, odd, t)
                down(step, k + 5, 1 - odd, 1, t - 1, rounds=rounds)

            gather(0, 0)
            gather(0, 1)
            pe.wait_ge(xe_split, 1)
            turn_selection()
            with pe.Fori(0, N_EXP) as g:
                expert_step(g, g)
            scatter(over_steps(pe, expert_step))
            norms[0] += 1
            pe.wait_ge(norm_squares, norms[0])
            for c in range(KC):
                mm = pe.matmul(M[:, 0:T], ones, area(A_SQ, KC, T)[:, c, :], start=(c == 0), stop=(c == KC - 1))
            mm.then_inc(norm_sum, 1)


def lay_out(inputs):
    f = {k: np.asarray(v) for k, v in inputs.items()}

    def channels(v):
        return v.reshape(-1, P).T

    vecs = []
    for layer in range(DEPTH):
        for name in VECS:
            if name == "conv_dw":
                w = f[name][layer].reshape(TAPS, 4, P)
                vecs.append(w.transpose(2, 1, 0).reshape(P, 4 * TAPS))
            else:
                vecs.append(channels(f[name][layer]))
    vecs.append(channels(f["c"][0]))

    def rows(w, chunks):
        return w.reshape(chunks, P, -1).transpose(1, 0, 2).reshape(P, WORDS)

    stream = np.empty((N_UNITS, P, WORDS), np.float32)
    cols = z_columns()
    branch = ("w_conv_out", "w_sb_out", "w_gla_out")
    for n, (kind, layer, a, b) in enumerate(PLAN):
        if kind == "ada":
            stream[n] = f["ada_w"][layer][P * b:P * b + P, WORDS * a:WORDS * a + WORDS]
        elif kind == "z":
            c = cols[a][0]
            stream[n] = rows(f["w_in"][layer][:, c:c + 256], KC)
        elif kind == "out":
            stream[n] = rows(f[branch[a]][layer][:, 512 * b:512 * b + 512], 4)
        elif kind == "wo":
            stream[n] = rows(f["w_o"][layer][:, 256 * a:256 * a + 256], KC)
        elif kind == "gate":
            stream[n] = rows(f["ffn_w_gate"][0][:, 256 * a:256 * a + 256], KC)
        elif kind == "up":
            stream[n] = rows(f["ffn_w_up"][0][:, 256 * a:256 * a + 256], KC)
        else:
            stream[n] = rows(f["ffn_w_down"][0][256 * a:256 * a + 256, :], 2)

    experts = np.empty((N_EXP, EU, P, WORDS), np.float32)
    for e in range(N_EXP):
        def pair(w, t):
            c = w[:, 512 * t:512 * t + 512]
            return [rows(c[512 * h:512 * h + 512], 4) for h in range(2)]

        def downs(t):
            w = f["moe_w_down"][0, e]
            return [rows(w[512 * t + 256 * h:512 * t + 256 * h + 256], 2) for h in range(2)]

        units = []
        for t in range(FT):
            units += pair(f["moe_w_gate"][0, e], t) + pair(f["moe_w_up"][0, e], t)
            if t:
                units += downs(t - 1)
        units += downs(FT - 1)
        experts[e] = units

    def turned(v):
        return v.T.reshape(KC, P, T).transpose(1, 0, 2)

    return {
        "x_t": turned(f["x"][0]),
        "vecs": np.concatenate(vecs, axis=1),
        "glr_w": f["w_in"][:, :, O_LR:O_LR + RANK].reshape(DEPTH, KC, P, RANK).transpose(0, 2, 1, 3),
        "a2": f["gla_a2"],
        "router": f["router_w"][0].reshape(KC, P, N_EXP).transpose(1, 0, 2),
        "stream": stream,
        "experts": experts.reshape(N_EXP * EU, P, WORDS),
    }


def kernel(**inputs):
    import concourse.bacc as bacc
    from concourse.bass_utils import run_bass_kernel_spmd

    nc = bacc.Bacc("TRN2", target_bir_lowering=False, num_devices=1)
    arrays, args = {}, {}
    for name, a in lay_out(inputs).items():
        a = np.ascontiguousarray(a)
        arrays[f"in_{name}"] = a
        args[name] = nc.dram_tensor(f"in_{name}", a.shape, mybir.dt.from_np(a.dtype), kind="ExternalInput").ap()
    args["out_t"] = nc.dram_tensor("out_t", (P, KC, T), F32, kind="ExternalOutput").ap()
    program(nc, **args)
    result = run_bass_kernel_spmd(nc, [arrays], core_ids=[0]).results[0]["out_t"]
    return np.ascontiguousarray(result.transpose(1, 0, 2).reshape(D, T).T)[None]
```

```python
from contextlib import ExitStack

import concourse.bass as bass
import numpy as np
from concourse import mybir

F32 = mybir.dt.float32
F32R = mybir.dt.float32r
I32 = mybir.dt.int32
U32 = mybir.dt.uint32
ALU = mybir.AluOpType
ACT = mybir.ActivationFunctionType

P = 128
D = 1024
T = 256
DEPTH = 2
KC = D // P
CONV = 512
TAPS = 31
SB_HEADS, SB_DH = 8, 64
GLA_HEADS, GLA_D = 4, 128
CH = 64
RANK = 16
D_FF = 2816
N_EXP = 8
D_FFE = 3584
EPS = 1e-6

WORDS = 2048
RAW = 6
SPLIT = 2
LAG = 2
WBANKS = 3
FT = D_FFE // 512
EU = 6 * FT

Z_UNITS = 18
G_UNITS = 12
PAIRS = D_FF // 256

O_SB = 2 * CONV
O_GLA = O_SB + 3 * 512
O_LR = O_GLA + 4 * 512
O_GATES = O_LR + RANK


def z_columns():
    cols = [(CONV, False), (0, False), (CONV + 256, False), (256, False)]
    for part in range(3):
        cols += [(O_SB + 512 * part + 256 * h, part == 2) for h in range(2)]
    for part in range(4):
        cols += [(O_GLA + 512 * part + 256 * h, part == 2) for h in range(2)]
    cols += [(O_GATES + 256 * u, False) for u in range(G_UNITS)]
    return cols


def plan():
    units = [("ada", 0, 0, k) for k in range(KC)]
    for layer in range(DEPTH):
        later = [("ada", 0, g, k) for g in (1, 2) for k in range(KC)] if layer == 0 else []
        for u in range(Z_UNITS + G_UNITS):
            units.append(("z", layer, u, 0))
            if later and (u < 9 or u % 2):
                units.append(later.pop(0))
        units += [("out", layer, b, h) for b in (1, 0, 2) for h in range(2)]
        units += [("wo", layer, q, 0) for q in range(4)]
        if layer == 0:
            later = [("ada", 1, g, k) for g in range(3) for k in range(KC)]
            for t in range(PAIRS + 1):
                if t < PAIRS:
                    units += [("gate", 0, t, 0)] + later[:1] + [("up", 0, t, 0)] + later[1:2]
                    later = later[2:]
                if t:
                    units += [("down", 0, t - 1, 0)] + later[:1]
                    later = later[1:]
    return units


PLAN = plan()
N_UNITS = len(PLAN)
W_UNITS = [u for u in PLAN if u[0] != "ada"]
N_W = len(W_UNITS)
POS = {u: n for n, u in enumerate(PLAN)}
WPOS = {u: n for n, u in enumerate(W_UNITS)}


def ahead(i, n):
    if i < 3:
        return [i]
    return [j for j in ((i, i + 1) if i == 3 else (i + 1,)) if j < n]


def slots():
    slot, freed, last = {}, {}, [-1] * 4
    for w, u in enumerate(W_UNITS):
        if u[0] == "z" and u[2] < 28:
            own = (0, 1, 2)
            if u[2] == 0:
                last[2] = w - 1
        elif u[0] in ("z", "out"):
            own = (0, 1)
        else:
            own = (0, 1, 3)
            if u[:1] + u[2:3] == ("wo", 0):
                last[3] = w - 1
        slot[u] = min(own, key=lambda i: last[i])
        freed[u] = last[slot[u]] + 1
        last[slot[u]] = w
    return slot, freed


SLOT, FREED = slots()
MOE_SLOTS = [SLOT[u] for u in W_UNITS[-3:]]
assert len(set(MOE_SLOTS)) == 3

VECS = {}
_at = 0
for _name, _n in (("mix_pre_g", 8), ("mix_post_g", 8), ("ffn_pre_g", 8), ("ffn_post_g", 8),
                  ("ada_b", 48), ("gla_a_b", 4), ("conv_dw_b", 4), ("conv_ln_g", 4),
                  ("conv_ln_b", 4), ("gla_norm_g", 4), ("conv_dw", 4 * TAPS)):
    VECS[_name] = (_at, _n)
    _at += _n
V_LAYER = _at
N_VEC = DEPTH * V_LAYER + KC

A_X = 0
A_H = A_X + 2048
A_GATES = A_H + 2048
A_Y = A_GATES + 6144
YW = TAPS - 1 + T
A_SQ = A_Y + 4 * YW
A_SK = A_SQ + 1024
A_SV = A_SK + 1024
A_GQ = A_SV + 1024
A_GK = A_GQ + 1024
A_GV = A_GK + 1024
A_GG = A_GV + 1024
A_ST = A_GG + 1024
A_CONST = A_ST + 2048
C_ID, C_ONES, C_LNEG, C_NEG = (A_CONST + P * i for i in range(4))
C_RS = A_CONST + 4 * P
C_RT = C_RS + T
C_MOD = C_RT + T
C_VEC = C_MOD + DEPTH * 80
C_COND = C_VEC + N_VEC
C_DEC = C_COND + KC
C_EPS = C_DEC + 16
A_END = C_EPS + 8


def program(nc, x_t, vecs, glr_w, a2, router, stream, experts, out_t):
    with ExitStack() as ctx:
        def sb(name, shape, dt=F32):
            return ctx.enter_context(nc.sbuf_tensor(name, shape, dt))

        def sem(name):
            return ctx.enter_context(nc.semaphore(name))

        raw = sb("raw", [P, RAW, WORDS])
        w_hi2 = sb("w_hi", [P, SPLIT, WORDS], F32R)
        w_lo2 = sb("w_lo", [P, SPLIT, WORDS], F32R)
        ar = sb("arena", [P, A_END])
        acts = sb("acts", [P, 10240], F32R)
        w_hi = [w_hi2[:, 0, :], w_hi2[:, 1, :], acts[:, 4096:6144], acts[:, 6144:8192]]
        w_lo = [w_lo2[:, 0, :], w_lo2[:, 1, :], acts[:, 8192:10240], acts[:, 8192:10240]]
        ints = sb("ints", [P, 24], I32)
        bank = [ctx.enter_context(nc.psum_tensor(f"bank{i}", [P, 512], F32)) for i in range(8)]
        WB = bank[0:3]
        Z = bank[3:5]
        O = bank[5:7]
        M = bank[7]

        def area(at, *dims):
            n = int(np.prod(dims))
            v = ar[:, at:at + n]
            if len(dims) == 2:
                return v.rearrange("p (a b) -> p a b", a=dims[0])
            if len(dims) == 3:
                return v.rearrange("p (a b c) -> p a b c", a=dims[0], b=dims[1])
            return v

        def split_area(at, *dims):
            n = int(np.prod(dims))
            if len(dims) == 1:
                return acts[:, at:at + n]
            return acts[:, at:at + n].rearrange("p (a b) -> p a b", a=dims[0])

        def f32(ap):
            return ap.bitcast(F32)

        x = area(A_X, KC, T)
        hf = area(A_H, KC, T)
        gates = area(A_GATES, 24, T)
        ada_acc = {(0, 0): area(A_GATES, 2048), (0, 1): area(A_GATES, 2048),
                   (0, 2): area(A_GATES + 2048, 2048), (1, 0): area(A_GATES + 4096, 2048),
                   (1, 1): area(A_GQ, 2048), (1, 2): area(A_GV, 2048)}
        y = area(A_GATES, KC, T)
        squares = area(A_GATES + 2048, KC, T)
        wglr = area(A_GATES + 4096, KC, RANK)
        a2_sb = area(A_GATES + 4096 + 128, 512)
        glr = area(A_GATES + 4096 + 640, T)
        ypad = area(A_Y, 4, YW)
        sq, sk, sv = area(A_SQ, 4, T), area(A_SK, 4, T), area(A_SV, 2, 512)
        gq, gk, gv, gg = area(A_GQ, 4, T), area(A_GK, 4, T), area(A_GV, 2, 512), area(A_GG, 4, T)
        conv_acc, conv_tmp = area(A_H, 4, T), area(A_H + 1024, 4, T)
        sig = area(A_ST, 2, T)
        stick_e = [area(A_ST + 512 * i, 2, T) for i in range(2)]
        stick_s = [area(A_ST + 1024 + 512 * i, 2, T) for i in range(2)]
        cum, gap, e_in, e_out = area(A_SQ, 4, T), area(A_SK, 4, T), area(A_SV, 4, T), area(A_ST, 4, T)
        ket, s_t = area(A_GK, 1024), area(A_GQ, 1024)
        states = [area(A_SQ, 512), area(A_SQ + 512, 512), area(A_ST + 1024, 512)]
        gla_o, gla_sq, gla_rs = area(A_SK, 4, T), area(A_ST, 4, T), area(A_SQ, 4, T)
        ident, ones = area(C_ID, P), area(C_ONES, P)
        l_neg, neg = area(C_LNEG, P), area(C_NEG, P)
        rs, rt = area(C_RS, T), area(C_RT, T)
        cond = area(C_COND, KC)
        decay = area(C_DEC, 4, 4)
        eps = area(C_EPS, 8)[:, 0:1]

        def mod(layer, i):
            at = C_MOD + 80 * layer + 8 * i
            return ar[:, at:at + 8]
        SH_M, SC_M, G_M, SH_F, SC_F, G_F, A_M, P_M, A_F, P_F = range(10)

        def vec(layer, name):
            at, n = VECS[name]
            at += C_VEC + V_LAYER * layer
            return ar[:, at:at + n]

        h_hi, h_lo = split_area(0, KC, T), split_area(2048, KC, T)
        br_hi = [split_area(4096 + 2048 * b, 4, T) for b in range(3)]
        br_lo = [split_area(4096 + 2048 * b + 1024, 4, T) for b in range(3)]
        ff_hi = [split_area(4096 + 1024 * b, 2, T) for b in range(2)]
        ff_lo = [split_area(4096 + 1024 * b + 512, 2, T) for b in range(2)]
        silu_g = [area(A_Y, 2, T), area(A_Y + 512, 2, T)]
        prod = [area(A_SQ, 2, T), area(A_SQ + 512, 2, T)]

        def bcast(row, n):
            return row.unsqueeze(1).to_broadcast([P, n, T])

        h_tok = area(A_GATES, 2 * D)
        moe_y = area(A_GATES + 2048, KC * T)
        y_e = area(A_GATES + 4096, D)
        silu_e = [area(A_GATES + 5120 + 512 * i, 512) for i in range(2)]
        act_e = [area(A_SQ + 512 * i, 512) for i in range(2)]
        sel, sel_w, sel_t = area(A_SK, T), area(A_SK + 256, T), area(A_SK + 512, T)
        iota, tril = area(A_SK + 768, P), area(A_SK + 896, P)
        logits, top = area(A_GQ, 16), area(A_GQ + 16, 2, 8)
        index_f, iota8 = area(A_GQ + 32, 2, 8), area(A_GQ + 48, 8)
        pick, pick_f = area(A_GQ + 56, 2, 8), area(A_GQ + 56, 16)
        comb, comb_f = area(A_GQ + 72, 2, 8), area(A_GQ + 72, 16)
        places, chosen, weights = (area(A_GQ + 512 + 32 * i, 2, 16) for i in range(3))
        places_f, chosen_f, weights_f = (area(A_GQ + 512 + 32 * i, 32) for i in range(3))
        column_f = area(A_GQ + 608, 12)
        prob, pick2 = area(A_GQ + 120, 2, 2), area(A_GQ + 124, 2, 8)
        over, place8 = area(A_GQ + 140, 8), area(A_GQ + 148, 8)
        list_f, hits = area(A_GQ + 156, 8), area(A_GQ + 164, 8)
        router_sb = area(A_GQ + 256, KC, N_EXP)
        index = sb("index", [P, 2, 8], U32)
        xe_hi, xe_lo = split_area(0, KC * P), split_area(1024, KC * P)
        ae_hi = [split_area(4096 + 1024 * b, 512) for b in range(2)]
        ae_lo = [split_area(4096 + 1024 * b + 512, 512) for b in range(2)]
        merged = area(A_H, KC, T)

        def flat(buffer):
            return buffer.rearrange("p a b -> p (a b)")[:, 0:384]

        SCATTER = (bank[2], bank[3], bank[7], bank[4])
        FB = Z + O
        ADA_TURN = (3, 6, 9)

        loaded = [sem(f"unit_loaded_{i}") for i in range(RAW)]
        hi_written = sem("hi_written")
        lo_written = sem("lo_written")
        released = sem("raw_slot_released")
        consumed = sem("unit_consumed")
        bank_read = [sem(f"bank_read_{i}") for i in range(7)]
        x_loaded, vec_loaded, lr_loaded = sem("x_loaded"), sem("vectors_loaded"), sem("low_rank_loaded")
        router_loaded = sem("router_loaded")
        consts, pad_zeroed = sem("constants_written"), sem("pad_zeroed")
        cond_ready = sem("cond_ready")
        ada_summed, ada_reduced, mods_ready = sem("ada_summed"), sem("ada_reduced"), sem("mods_ready")
        dve_step, act_step, pool_step = sem("dve_step"), sem("act_step"), sem("pool_step")
        norm_squares, norm_sum, norm_root = sem("norm_squares"), sem("norm_sum"), sem("norm_root")
        h_scaled, h_ready, h_split = sem("h_scaled"), sem("h_ready"), sem("h_split")
        lr_ready, lr_copied = sem("low_rank_ready"), sem("low_rank_copied")
        z_ready, ln_ready, sp_ready, sp_masked = (sem("stick_z_ready"), sem("stick_ln_ready"),
                                                  sem("stick_sp_ready"), sem("stick_sp_masked"))
        arg_ready, att_ready, att_masked, o_ready = (sem("stick_arg_ready"), sem("stick_att_ready"),
                                                     sem("stick_att_masked"), sem("stick_o_ready"))
        o_split = sem("stick_o_split")
        la_ready, la_read, soft_ready = sem("log_a_ready"), sem("log_a_read"), sem("softplus_ready")
        cum_ready, exp_ready, dec_ready = sem("cumulated"), sem("exponentials_ready"), sem("decayed_ready")
        ke_ready, sc_ready, ke_copied, sc_copied = (sem("k_end_turned"), sem("gla_scores_ready"),
                                                    sem("k_end_copied"), sem("gla_scores_copied"))
        sc_masked, ds_ready, st_ready = sem("gla_scores_masked"), sem("d_state_ready"), sem("states_ready")
        go_ready, go_copied, gs_ready = sem("gla_o_ready"), sem("gla_o_copied"), sem("gla_sums_ready")
        gr_ready = sem("gla_roots_ready")
        conv_done, mean_ready, mean_copied, centred = (sem("conv_done"), sem("conv_mean_ready"),
                                                       sem("conv_mean_copied"), sem("conv_centred"))
        cv_squared, var_ready, cv_root, cv_scaled = (sem("conv_squared"), sem("conv_var_ready"),
                                                   sem("conv_root_ready"), sem("conv_scaled"))
        cv_silu, gg_silu, gates_ready = sem("conv_silu_ready"), sem("gg_silu_ready"), sem("gates_ready")
        a_split, c_split, s_split = sem("conv_split"), sem("gla_split"), sem("merged_split")
        merged_pair, merged_hi = sem("merged_pair"), sem("merged_high")
        y_copied, x_updated = sem("y_copied"), sem("x_updated")
        ff_split, down_copied = sem("ffn_split"), sem("ffn_down_copied")
        stored = sem("output_stored")
        conv_taps, pool_taps, scans = sem("conv_taps"), sem("pool_conv_taps"), sem("scans")
        pool_products = sem("pool_conv_products")
        htok_turned, htok_copied = sem("h_turned"), sem("h_tok_copied")
        logits_done, gap_ready, exp_done = sem("logits_done"), sem("logit_gap_ready"), sem("router_exp_done")
        routed, counted, list_ready = sem("routed"), sem("tokens_counted"), sem("overflow_list_ready")
        moe_consts = sem("moe_constants_written")
        sel_ready, sel_turned = sem("selection_ready"), sem("selection_turned")
        gathered, xe_hi_done, xe_split = sem("gathered"), sem("expert_input_high"), sem("expert_input_split")
        silu_done, act_done, turned = sem("silu_done"), sem("act_done"), sem("act_turned")
        ae_hi_done, ae_split = sem("act_high"), sem("act_split")
        ye_copied, scattered, moe_added = sem("expert_y_copied"), sem("scattered"), sem("moe_added")
        sel_zeroed, sel_w_ready = sem("selection_zeroed"), sem("weighted_selection_ready")

        block = ctx.enter_context(nc.Block())

        def mixer_units(layer):
            return [u for u in W_UNITS if u[1] == layer and u[0] in ("z", "out", "wo")]

        def mixer_place(u):
            return mixer_units(u[1]).index(u)

        BANKS = {}
        used = [0] * 7
        turn_of = 0
        for u in W_UNITS:
            if u[0] == "out" and mixer_place(u) % 3 != 1:
                at = (5, 6) if mixer_place(u) % 3 == 0 else (3, 4)
            else:
                n = {"out": 2, "down": 0}.get(u[0], 1)
                at = [(turn_of + j) % WBANKS for j in range(n)]
                turn_of += n
            BANKS[u] = [(b, used[b]) for b in at]
            for b in at:
                used[b] += 1

        FFN_UNITS = [u for u in W_UNITS if u[0] in ("gate", "up", "down")]

        def two(ap):
            return ap.rearrange("p (a b) -> p a b", a=2)

        def wait_read(eng, u):
            for b, before in BANKS[u]:
                eng.wait_ge(bank_read[b], before + 1)

        def moe_unit(step, k, rounds=0):
            n, w = N_UNITS + k, N_W + k
            landed = step * (16 * EU // RAW) + rounds * 16 + 16 * (n // RAW + 1)
            return n % RAW, landed, MOE_SLOTS[k % 3], step * EU + rounds * RAW + w

        def over_steps(eng, body):
            eng.wait_ge(list_ready, 1)
            n = eng.value_load(ints[0:1, 0:1], min_val=0, max_val=3)
            with eng.If(n > 0):
                with eng.Fori(0, n) as j:
                    expert = eng.value_load(ints[0:1, bass.ds(j + 1, 1)], min_val=0, max_val=N_EXP - 1)
                    body(j + N_EXP, expert)
                eng.nop()
            return n + N_EXP

        @block.sync
        def _(sp):
            def load(n, value, src):
                sp.wait_ge(released, value)
                sp.dma_start(raw[:, n % RAW, :], src).then_inc(loaded[n % RAW], 16)

            sp.dma_start(ar[:, C_VEC:C_VEC + N_VEC], vecs).then_inc(vec_loaded, 16)
            for n in range(RAW):
                sp.dma_start(raw[:, n, :], stream[n]).then_inc(loaded[n], 16)
                if n == 1:
                    sp.dma_start(x, x_t).then_inc(x_loaded, 16)
            rounds = (N_UNITS - RAW) // RAW
            with sp.Fori(0, rounds) as r:
                for s in range(RAW):
                    load(s, r * RAW + s + 1, stream[bass.ds(r * RAW + RAW + s, 1), :, :].rearrange(
                        "a p n -> p (a n)"))
            for n in range(RAW + rounds * RAW, N_UNITS):
                load(n, n - RAW + 1, stream[n])

            def expert_step(step, expert):
                with sp.Fori(0, EU // RAW) as q:
                    for s in range(RAW):
                        load(N_UNITS + s, step * EU + q * RAW + (N_UNITS + s - RAW + 1),
                             experts[bass.ds(expert * EU + q * RAW + s, 1), :, :].rearrange(
                                 "a p n -> p (a n)"))

            with sp.Fori(0, N_EXP) as g:
                expert_step(g, g)
            over_steps(sp, expert_step)
            sp.wait_ge(x_updated, 2 * DEPTH * KC)
            sp.dma_start(out_t, x).then_inc(stored, 16)
            sp.wait_ge(stored, 16)

        @block.gpsimd
        def _(pool):
            pool.memset(neg, -1.0).then_inc(consts, 1)
            pool.memset(ones, 1.0).then_inc(consts, 1)
            pool.memset(ar[:, C_EPS:C_EPS + 8], EPS).then_inc(consts, 1)
            pool.wait_ge(consts, 3)
            pool.affine_select(l_neg, neg, [[-1, P]], ALU.is_ge, 0.0, 0, 1).then_inc(consts, 1)
            pool.affine_select(ident, ones, [[-1, P]], ALU.is_equal, 0.0, 0, 1).then_inc(consts, 1)
            products = [0]

            def taps(layer, k0, k1):
                for k in range(k0, k1):
                    w = vec(layer, "conv_dw")[:, TAPS * 3 + k:TAPS * 3 + k + 1]
                    src, acc, product = ypad[:, 3, k:k + T], conv_acc[:, 3, :], conv_tmp[:, k % 2, :]
                    if k == 0:
                        pool.tensor_scalar(acc, src, w, vec(layer, "conv_dw_b")[:, 3:4],
                                           ALU.mult, ALU.add).then_inc(pool_taps, 1)
                        continue
                    if k > 1:
                        pool.wait_ge(pool_taps, TAPS * layer + k - 1)
                    pool.tensor_scalar(product, src, w, None, ALU.mult).then_inc(pool_products, 1)
                    products[0] += 1
                    pool.wait_ge(pool_products, products[0])
                    pool.wait_ge(pool_taps, TAPS * layer + k)
                    pool.tensor_tensor(acc, acc, product, ALU.add).then_inc(pool_taps, 1)

            for layer in range(DEPTH):
                if layer:
                    pool.wait_ge(ada_reduced, 6)
                    pool.wait_ge(ff_split, PAIRS)
                pool.dma_start(wglr, glr_w[layer]).then_inc(lr_loaded, 16)
                pool.dma_start(a2_sb[0:RANK, :], a2[layer]).then_inc(lr_loaded, 16)
                pool.memset(ypad[:, :, 0:TAPS - 1], 0.0).then_inc(pad_zeroed, 1)
                wait_read(pool, ("z", layer, 3, 0))
                taps(layer, 0, 20)
                for i in range(SB_HEADS + 1):
                    if i < SB_HEADS:
                        s = stick_s[i % 2][:, :, 0:P]
                        pool.wait_ge(sp_ready, layer * SB_HEADS + i + 1)
                        pool.affine_select(s, s, [[0, 2], [1, P]], ALU.is_gt, 0.0, 0, -1).then_inc(sp_masked, 1)
                    if i:
                        e = stick_e[(i - 1) % 2][:, :, 0:P]
                        pool.wait_ge(att_ready, layer * SB_HEADS + i)
                        pool.affine_select(e, e, [[0, 2], [1, P]], ALU.is_gt, 0.0, 0, -1).then_inc(att_masked, 1)
                taps(layer, 20, TAPS)
                pool.wait_ge(sc_copied, 2 * (layer + 1))
                both = area(A_GQ, 8, P)
                pool.affine_select(both, both, [[0, 8], [1, P]], ALU.is_ge, 0.0, 0, -1).then_inc(pool_step, 1)
                pool.wait_ge(pool_step, layer + 1)
                pool.memset(both[0:CH, :, CH:P], 0.0).then_inc(sc_masked, 1)
            pool.wait_ge(c_split, DEPTH)
            pool.dma_start(router_sb, router).then_inc(router_loaded, 16)
            pool.iota(iota, [[1, P]], 0, 0, allow_small_or_imprecise_dtypes=True).then_inc(moe_consts, 1)
            pool.iota(iota8, [[1, 8]], 0, 0, allow_small_or_imprecise_dtypes=True).then_inc(moe_consts, 1)
            pool.affine_select(tril, ones, [[1, P]], ALU.is_gt, 0.0, 0, -1).then_inc(moe_consts, 1)

        @block.scalar
        def _(act):
            steps, norms = [0], [0]

            def link(ins):
                steps[0] += 1
                ins.then_inc(act_step, 1)
                act.wait_ge(act_step, steps[0])

            def write_hi(u):
                slot = POS[u] % RAW
                act.wait_ge(loaded[slot], 16 * (POS[u] // RAW + 1))
                if FREED[u]:
                    act.wait_ge(consumed, FREED[u])
                act.activation(w_hi[SLOT[u]], raw[:, slot, :], ACT.Copy).then_inc(hi_written, 1)

            def root(to, sums, n, done):
                act.activation(to, sums, ACT.Sqrt, bias=eps, scale=1.0 / n).then_inc(done, 1)

            def norm(sums=M):
                norms[0] += 1
                act.wait_ge(norm_sum, norms[0])
                root(rt, sums[:, 0:T], D, norm_root)

            def norm_x(updates):
                for q in range(4):
                    if updates:
                        act.wait_ge(x_updated, KC * (updates - 1) + 2 * q + 2)
                    act.activation(squares[:, 2 * q:2 * q + 2, :], x[:, 2 * q:2 * q + 2, :],
                                   ACT.Square).then_inc(norm_squares, 1)
                norm()

            def shift(layer, b, count, split_too=True):
                for c in range(KC):
                    act.wait_ge(h_scaled, KC * (count - 1) + c + 1)
                    bias = mod(layer, b)[:, c:c + 1]
                    if split_too:
                        act.activation(h_hi[:, c, :], hf[:, c, :], ACT.Identity, bias=bias)
                    act.activation(hf[:, c, :], hf[:, c, :], ACT.Identity, bias=bias).then_inc(h_ready, 1)

            def merged_high(layer, half):
                for q in (2 * half, 2 * half + 1):
                    act.wait_ge(merged_pair, 4 * layer + q + 1)
                    act.activation(h_hi[:, 2 * q:2 * q + 2, :], merged[:, 2 * q:2 * q + 2, :],
                                   ACT.Copy).then_inc(merged_hi, 1)

            def copy_unit(u, to, func=ACT.Copy, scale=1.0):
                act.wait_ge(consumed, WPOS[u] + 1)
                b = BANKS[u][0][0]
                act.activation(to, two(bank[b]), func, scale=scale).then_inc(bank_read[b], 1)

            neg_b = area(C_DEC, 16)[:, 0:4]

            def evacuate(layer, i, u):
                if u[0] == "z" and i in (0, 2):
                    if i == 2:
                        wait_read(act, ("z", layer, 1, 0))
                    copy_unit(u, sig, ACT.Sigmoid)
                elif u[0] == "z" and 4 <= i < 10:
                    part, h = divmod(i - 4, 2)
                    to = sv[:, :, 256 * h:256 * h + 256] if part == 2 else (sq, sk)[part][:, 2 * h:2 * h + 2, :]
                    copy_unit(u, to, scale=SB_DH ** -0.5 if part == 0 else 1.0)
                elif u[0] == "z" and 10 <= i < Z_UNITS:
                    part, h = divmod(i - 10, 2)
                    to = gv[:, :, 256 * h:256 * h + 256] if part == 2 else \
                        (gq, gk, None, gg)[part][:, 2 * h:2 * h + 2, :]
                    copy_unit(u, to, scale=GLA_D ** -0.5 if part == 0 else 1.0)
                elif u[0] == "z" and i >= Z_UNITS:
                    j = i - Z_UNITS
                    if j in (0, 4) and layer == 0:
                        act.wait_ge(ada_reduced, 2 + j // 4)
                    if j == 8:
                        act.wait_ge(la_ready, 2 * layer + 2)
                    copy_unit(u, gates[:, 2 * j:2 * j + 2, :])
                elif u[0] == "wo":
                    if i == 36:
                        act.wait_ge(s_split, 4 * (layer + 1))
                    q = i - 36
                    act.wait_ge(consumed, WPOS[u] + 1)
                    act.activation(squares[:, 2 * q:2 * q + 2, :], two(bank[BANKS[u][0][0]]),
                                   ACT.Square).then_inc(norm_squares, 1)
                    copy_unit(u, y[:, 2 * q:2 * q + 2, :])

            def stick_ln(layer, hh):
                n = layer * SB_HEADS + hh
                e = flat(stick_e[hh % 2])
                act.wait_ge(z_ready, n + 1)
                if hh >= 2:
                    act.wait_ge(o_ready, n - 1)
                else:
                    wait_read(act, ("z", layer, 3, 0))
                link(act.activation(e, Z[hh % 2][:, 0:384], ACT.Abs))
                link(act.activation(e, e, ACT.Exp, scale=-1.0))
                act.activation(e, e, ACT.Ln, bias=1.0).then_inc(ln_ready, 1)

            def stick_att(layer, hh):
                act.wait_ge(arg_ready, layer * SB_HEADS + hh + 1)
                act.activation(flat(stick_e[hh % 2]), Z[hh % 2][:, 0:384], ACT.Exp).then_inc(att_ready, 1)

            def log_a(layer, half):
                act.wait_ge(la_ready, 2 * layer + half + 1)
                if half == 0:
                    act.wait_ge(z_ready, SB_HEADS * (layer + 1))
                for k in range(2):
                    h = 2 * half + k
                    act.activation(cum[:, h, :], M[:, T * k:T * k + T], ACT.Abs,
                                   bias=vec(layer, "gla_a_b")[:, h:h + 1]).then_inc(la_read, 1)
                    act.activation(gap[:, h, :], M[:, T * k:T * k + T], ACT.Relu,
                                   bias=neg_b[:, h:h + 1], scale=-1.0).then_inc(la_read, 1)

            def hook(layer, i):
                if i == 1:
                    if layer:
                        act.wait_ge(consumed, WPOS[FFN_UNITS[-1]] + 1)
                        for q in range(4):
                            act.activation(squares[:, 2 * q:2 * q + 2, :], two(FB[q]),
                                           ACT.Square).then_inc(norm_squares, 1)
                        for q in range(4):
                            act.activation(y[:, 2 * q:2 * q + 2, :], two(FB[q]), ACT.Copy).then_inc(down_copied, 1)
                        norm()
                        norm_x(2 * layer)
                    shift(layer, SH_M, 2 * layer + 1)
                    act.activation(neg_b, vec(layer, "gla_a_b"), ACT.Copy, scale=-1.0).then_inc(lr_copied, 1)
                if i == 2:
                    act.wait_ge(lr_ready, layer + 1)
                    act.activation(glr[0:RANK, :], M[0:RANK, 0:T], ACT.Copy).then_inc(lr_copied, 1)
                if 0 <= i - 12 < SB_HEADS:
                    stick_att(layer, i - 12)
                if 0 <= i - 11 < SB_HEADS:
                    stick_ln(layer, i - 11)
                if i == 20:
                    log_a(layer, 0)
                if i == 21:
                    log_a(layer, 1)
                    act.wait_ge(la_read, 8 * (layer + 1))
                    link(act.activation(cum, cum, ACT.Exp, scale=-1.0))
                    act.activation(cum, cum, ACT.Ln, bias=1.0).then_inc(soft_ready, 1)
                if i == 22:
                    act.wait_ge(cum_ready, layer + 1)
                    act.wait_ge(o_ready, SB_HEADS * (layer + 1))
                    act.activation(e_in, cum, ACT.Exp, scale=-1.0 / 16).then_inc(exp_ready, 1)
                    act.activation(e_out, cum, ACT.Exp, scale=1.0 / 16).then_inc(exp_ready, 1)
                    act.activation(gap, gap, ACT.Exp, scale=-1.0 / 16).then_inc(exp_ready, 1)
                if i == 24:
                    act.wait_ge(dec_ready, layer + 1)
                    for t in range(2):
                        act.wait_ge(ke_ready, 2 * layer + t + 1)
                        act.activation(ket[:, 512 * t:512 * t + 512], Z[t][:, :], ACT.Copy).then_inc(ke_copied, 1)
                    for t in range(2):
                        act.wait_ge(sc_ready, 2 * layer + t + 1)
                        act.activation(s_t[:, 512 * t:512 * t + 512], O[t][:, :], ACT.Copy).then_inc(sc_copied, 1)
                if i == 26:
                    for t in range(2):
                        act.wait_ge(go_ready, 2 * layer + t + 1)
                        act.activation(gla_o[:, 2 * t:2 * t + 2, :], two(O[t]), ACT.Copy).then_inc(go_copied, 1)
                        act.activation(gla_sq[:, 2 * t:2 * t + 2, :], two(O[t]), ACT.Square).then_inc(go_copied, 1)
                if i == 27:
                    act.wait_ge(gs_ready, 2 * (layer + 1))
                    root(gla_sq[:, 0:2, :], two(M), GLA_D, gr_ready)
                    root(gla_sq[:, 2:4, :], two(Z[0]), GLA_D, gr_ready)
                    act.wait_ge(mean_ready, layer + 1)
                    act.activation(rt, Z[1][:, 0:T], ACT.Copy, scale=1.0 / CONV).then_inc(mean_copied, 1)
                if i == 28:
                    act.wait_ge(centred, layer + 1)
                    act.activation(conv_tmp, conv_acc, ACT.Square).then_inc(cv_squared, 1)
                if i == 29:
                    act.wait_ge(var_ready, layer + 1)
                    root(rt, Z[1][:, 0:T], CONV, cv_root)
                if i == 30:
                    act.wait_ge(cv_scaled, layer + 1)
                    for c in range(4):
                        act.activation(conv_tmp[:, c, :], conv_acc[:, c, :], ACT.Silu,
                                       bias=vec(layer, "conv_ln_b")[:, c:c + 1],
                                       scale=vec(layer, "conv_ln_g")[:, c:c + 1]).then_inc(cv_silu, 1)
                    act.activation(gg, gg, ACT.Silu).then_inc(gg_silu, 1)
                if i == 31:
                    for j in range(3):
                        wait_read(act, ("z", layer, Z_UNITS + G_UNITS - 1 - j, 0))
                if i in (31, 32, 34):
                    b = {31: 1, 32: 0, 34: 2}[i]
                    g = gates[:, 8 * b:8 * b + 8, :]
                    act.activation(g, g, ACT.Sigmoid).then_inc(gates_ready, 1)
                if i in (36, 37):
                    merged_high(layer, i - 36)

            def mixer_norms(layer):
                norm()
                norm_x(2 * layer + 1)
                shift(layer, SH_F, 2 * layer + 2, split_too=(layer == 0))

            act.wait_ge(vec_loaded, 16)
            act.activation(cond, ar[:, C_VEC + DEPTH * V_LAYER:C_VEC + N_VEC], ACT.Silu).then_inc(cond_ready, 1)
            act.wait_ge(consts, 5)
            act.wait_ge(x_loaded, 16)
            norm_x(0)
            for layer in range(DEPTH):
                units = mixer_units(layer)
                for i in range(len(units)):
                    for j in ahead(i, len(units)):
                        write_hi(units[j])
                    if i >= LAG:
                        evacuate(layer, i - LAG, units[i - LAG])
                    hook(layer, i)
                if layer == 0:
                    for i, u in enumerate(FFN_UNITS):
                        if i < LAG:
                            evacuate(layer, 38 + i, units[38 + i])
                        write_hi(u)
                        if i >= LAG:
                            b = FFN_UNITS[i - LAG]
                            if b[0] == "gate":
                                if b[2] >= 2:
                                    act.wait_ge(ff_split, b[2] - 1)
                                copy_unit(b, silu_g[b[2] % 2], ACT.Silu)
                        if i == 1:
                            mixer_norms(layer)
                else:
                    for i in (38, 39):
                        evacuate(layer, i, units[i])
                    mixer_norms(layer)

            act.wait_ge(gap_ready, 1)
            act.activation(prob[:, :, 1], prob[:, :, 0], ACT.Exp).then_inc(exp_done, 1)
            for q in range(4):
                act.wait_ge(htok_turned, q + 1)
                act.activation(h_tok[:, 512 * q:512 * q + 512], (O[0], O[1], M, Z[1])[q][:, :],
                               ACT.Copy).then_inc(htok_copied, 1)

            def moe_hi(step, k, rounds=0):
                slot, landed, s, w = moe_unit(step, k, rounds)
                act.wait_ge(loaded[slot], landed)
                act.wait_ge(consumed, w - SPLIT)
                act.activation(w_hi[s], raw[:, slot, :], ACT.Copy).then_inc(hi_written, 1)

            def silu_tile(step, k, odd, rounds=0):
                act.wait_ge(consumed, moe_unit(step, k, rounds)[3] + 1)
                act.activation(silu_e[odd], bank[2 * odd][:, :], ACT.Silu).then_inc(silu_done, 1)

            def expert_step(step, expert):
                moe_hi(step, 0)
                moe_hi(step, 1)
                expert_result(step)
                moe_hi(step, 2)
                moe_hi(step, 3)
                silu_tile(step, 1, 0)
                with act.Fori(0, (FT - 1) // 2) as q:
                    for r in range(2):
                        for j in range(4):
                            moe_hi(step, 4 + 6 * r + j, q * 2)
                        silu_tile(step, 4 + 6 * r + 1, 1 - r, q * 2)
                        for j in range(4, 6):
                            moe_hi(step, 4 + 6 * r + j, q * 2)
                for k in (EU - 2, EU - 1):
                    moe_hi(step, k)

            def expert_result(step):
                act.wait_ge(sel_turned, step + 1)
                act.activation(sel_t, bank[7][:, 0:T], ACT.Copy).then_inc(ye_copied, 1)
                for half in range(2):
                    act.activation(y_e[:, 512 * half:512 * half + 512], bank[5 + half][:, :],
                                   ACT.Copy).then_inc(ye_copied, 1)

            with act.Fori(0, N_EXP) as g:
                expert_step(g, g)
            n_steps = over_steps(act, expert_step)
            expert_result(n_steps)
            for p in range(4):
                act.wait_ge(moe_added, n_steps * 4 + p + 1)
                act.activation(area(A_SQ + 512 * p, 512), moe_y[:, 512 * p:512 * p + 512],
                               ACT.Square).then_inc(norm_squares, 1)
            norm(O[0])

        @block.vector
        def _(dve):
            steps, norms = [0], [0]

            def link(ins):
                steps[0] += 1
                ins.then_inc(dve_step, 1)
                dve.wait_ge(dve_step, steps[0])

            def write_lo(u):
                w = WPOS[u]
                dve.wait_ge(hi_written, w + 1)
                dve.tensor_tensor(w_lo[SLOT[u]], raw[:, POS[u] % RAW, :], f32(w_hi[SLOT[u]]),
                                  ALU.subtract).then_inc(lo_written, 1)
                dve.wait_ge(lo_written, w + 1)
                dve.sem_inc(released, 1)

            def add_ada(u):
                _, layer, g, k = u
                n = POS[u]
                dve.wait_ge(loaded[n % RAW], 16 * (n // RAW + 1))
                acc = ada_acc[layer, g]
                w = raw[:, n % RAW, :]
                if k == 0:
                    if (layer, g) == (0, 1):
                        dve.wait_ge(ada_reduced, 1)
                    ins = dve.tensor_scalar(acc, w, cond[:, 0:1], None, ALU.mult)
                else:
                    ins = dve.scalar_tensor_tensor(acc, w, cond[:, k:k + 1], acc, ALU.mult, ALU.add)
                ins.then_inc(released, 1)
                dve.wait_ge(released, n + 1)
                if k == KC - 1:
                    dve.sem_inc(ada_summed, 1)

            def finish_mods(layer, g):
                dve.wait_ge(ada_reduced, 3 * layer + g + 1)
                at = C_MOD + 80 * layer + 16 * g
                link(dve.tensor_tensor(ar[:, at:at + 16], M[:, 16 * g:16 * g + 16],
                                       vec(layer, "ada_b")[:, 16 * g:16 * g + 16], ALU.add))
                if g == 0:
                    ins = dve.scalar_tensor_tensor(mod(layer, A_M), mod(layer, SC_M), 1.0,
                                                   vec(layer, "mix_pre_g"), ALU.add, ALU.mult)
                elif g == 1:
                    ins = dve.tensor_tensor(mod(layer, P_M), mod(layer, G_M), vec(layer, "mix_post_g"), ALU.mult)
                else:
                    link(dve.tensor_tensor(mod(layer, P_F), mod(layer, G_F), vec(layer, "ffn_post_g"), ALU.mult))
                    ins = dve.scalar_tensor_tensor(mod(layer, A_F), mod(layer, SC_F), 1.0,
                                                   vec(layer, "ffn_pre_g"), ALU.add, ALU.mult)
                ins.then_inc(mods_ready, 1)
                dve.wait_ge(mods_ready, 3 * layer + g + 1)

            def split(hi, lo, src, done, value):
                link(dve.tensor_copy(hi, src))
                dve.tensor_tensor(lo, src, f32(hi), ALU.subtract).then_inc(done, 1)
                dve.wait_ge(done, value)

            def reciprocal_rms():
                norms[0] += 1
                dve.wait_ge(norm_root, norms[0])
                link(dve.reciprocal(rs, rt))

            def norm_in(layer, a, count, split_too=True):
                if count > 1:
                    reciprocal_rms()
                for c in range(KC + 2):
                    if c < KC:
                        dve.scalar_tensor_tensor(hf[:, c, :], x[:, c, :], mod(layer, a)[:, c:c + 1], rs,
                                                 ALU.mult, ALU.mult).then_inc(h_scaled, 1)
                    if c >= 2 and split_too:
                        dve.wait_ge(h_ready, KC * (count - 1) + c - 1)
                        dve.tensor_tensor(h_lo[:, c - 2, :], hf[:, c - 2, :], f32(h_hi[:, c - 2, :]),
                                          ALU.subtract).then_inc(h_split, 1)

            def norm_out(src, layer, p, count):
                reciprocal_rms()
                for c in range(KC + 1):
                    if c < KC:
                        steps[0] += 1
                        dve.scalar_tensor_tensor(src[:, c, :], src[:, c, :], mod(layer, p)[:, c:c + 1], rs,
                                                 ALU.mult, ALU.mult).then_inc(dve_step, 1)
                    if c:
                        dve.wait_ge(dve_step, steps[0] - (c < KC))
                        dve.tensor_tensor(x[:, c - 1, :], x[:, c - 1, :], src[:, c - 1, :],
                                          ALU.add).then_inc(x_updated, 1)
                dve.wait_ge(x_updated, KC * count)

            def glu(layer, h):
                u = ("z", layer, 2 * h + 1, 0)
                wait_read(dve, ("z", layer, 2 * h, 0))
                dve.wait_ge(consumed, WPOS[u] + 1)
                dve.wait_ge(pad_zeroed, layer + 1)
                b, before = BANKS[u][0]
                dve.tensor_tensor(ypad[:, 2 * h:2 * h + 2, TAPS - 1:YW], two(bank[b]), sig,
                                  ALU.mult).then_inc(bank_read[b], 1)
                dve.wait_ge(bank_read[b], before + 1)

            taps_done = {}

            def taps(layer, i):
                for n in range(2):
                    for c in range(3):
                        first = (4, 4, 6)[c]
                        k = TAPS * (i - first) // (26 - first) + n
                        if i < first or k >= TAPS * (i - first + 1) // (26 - first):
                            continue
                        w = vec(layer, "conv_dw")[:, TAPS * c + k:TAPS * c + k + 1]
                        src, acc = ypad[:, c, k:k + T], conv_acc[:, c, :]
                        if k == 0:
                            ins = dve.tensor_scalar(acc, src, w, vec(layer, "conv_dw_b")[:, c:c + 1],
                                                    ALU.mult, ALU.add)
                        else:
                            dve.wait_ge(conv_taps, taps_done[c])
                            ins = dve.scalar_tensor_tensor(acc, src, w, acc, ALU.mult, ALU.add)
                        ins.then_inc(conv_taps, 1)
                        tap_count[0] += 1
                        taps_done[c] = tap_count[0]

            tap_count = [0]

            def stick_sp(layer, hh):
                n = layer * SB_HEADS + hh
                dve.wait_ge(ln_ready, n + 1)
                if hh >= 2:
                    dve.wait_ge(arg_ready, n - 1)
                dve.scalar_tensor_tensor(flat(stick_s[hh % 2]), Z[hh % 2][:, 0:384], 0.0,
                                         flat(stick_e[hh % 2]), ALU.max, ALU.add).then_inc(sp_ready, 1)

            def stick_out(layer, c):
                dve.wait_ge(o_ready, layer * SB_HEADS + 2 * c + 2)
                split(br_hi[1][:, c, :], br_lo[1][:, c, :], O[c % 2][:, 0:T], o_split, 4 * layer + c + 1)

            def gla_cum(layer):
                dve.wait_ge(soft_ready, layer + 1)
                link(dve.tensor_tensor(cum, cum, gap, ALU.add))
                for h in range(GLA_HEADS):
                    for c in range(4):
                        s = cum[:, h, CH * c:CH * c + CH]
                        ins = dve.tensor_tensor_scan(gap[:, h, CH * c:CH * c + CH], ones[:, 0:CH], s, 0.0,
                                                     ALU.mult, ALU.add)
                        ins.then_inc(scans, 1)
                dve.wait_ge(scans, 16 * (layer + 1))
                link(dve.tensor_copy(cum, gap))
                c4 = area(A_SQ, 16, CH)
                dve.tensor_tensor(area(A_SK, 16, CH), c4[:, :, CH - 1:CH].to_broadcast([P, 16, CH]), c4,
                                  ALU.subtract).then_inc(cum_ready, 1)

            def gla_decay(layer):
                dve.wait_ge(exp_ready, 3 * (layer + 1))
                link(dve.tensor_copy(area(C_DEC, 16), area(A_SV, 16, CH)[:, :, CH - 1]))
                link(dve.tensor_tensor(e_in, gq, e_in, ALU.mult))
                link(dve.tensor_tensor(gap, gk, gap, ALU.mult))
                dve.tensor_tensor(e_out, gk, e_out, ALU.mult).then_inc(dec_ready, 1)

            def gla_states(layer):
                for j in range(3):
                    src = (M, Z[0], Z[1])[j]
                    dve.wait_ge(ds_ready, 3 * layer + j + 1)
                    if j == 0:
                        ins = dve.tensor_copy(states[0], src[:, :])
                        link(ins)
                    else:
                        for h in range(GLA_HEADS):
                            c = P * h
                            ins = dve.scalar_tensor_tensor(states[j][:, c:c + P], states[j - 1][:, c:c + P],
                                                           decay[:, h, j:j + 1], src[:, c:c + P],
                                                           ALU.mult, ALU.add)
                            link(ins)
                dve.sem_inc(st_ready, 1)

            def gla_scale(layer):
                dve.wait_ge(gr_ready, 2 * (layer + 1))
                link(dve.reciprocal(gla_rs, gla_sq))
                for h in range(GLA_HEADS):
                    link(dve.scalar_tensor_tensor(gla_o[:, h, :], gla_o[:, h, :],
                                                  vec(layer, "gla_norm_g")[:, h:h + 1], gla_rs[:, h, :],
                                                  ALU.mult, ALU.mult))

            def merge(layer, i, u):
                _, _, b, half = u
                dve.wait_ge(consumed, WPOS[u] + 1)
                if half == 0:
                    dve.wait_ge(gates_ready, 3 * layer + 1 + (1, 0, 2).index(b))
                if i == 30:
                    dve.wait_ge(cv_silu, 4 * (layer + 1))
                for j in range(2):
                    q = 2 * half + j
                    bk, before = BANKS[u][j]
                    g = gates[:, 8 * b + 2 * q:8 * b + 2 * q + 2, :]
                    to = merged[:, 2 * q:2 * q + 2, :] if b == 1 else g
                    dve.tensor_tensor(to, two(bank[bk]), g, ALU.mult).then_inc(bank_read[bk], 1)
                if b == 1:
                    for bk, before in BANKS[u]:
                        dve.wait_ge(bank_read[bk], before + 1)
                    return
                for j in range(2):
                    q = 2 * half + j
                    bk, before = BANKS[u][j]
                    dve.wait_ge(bank_read[bk], before + 1)
                    m = merged[:, 2 * q:2 * q + 2, :]
                    ins = dve.tensor_tensor(m, m, gates[:, 8 * b + 2 * q:8 * b + 2 * q + 2, :], ALU.add)
                    if b == 2:
                        ins.then_inc(merged_pair, 1)
                    else:
                        link(ins)

            def hook(layer, i):
                if i == 1:
                    if layer == 0:
                        finish_mods(0, 0)
                    norm_in(layer, A_M, 2 * layer + 1)
                if layer == 0 and i == 12:
                    finish_mods(0, 1)
                if layer == 0 and i == 24:
                    finish_mods(0, 2)
                if 0 <= i - 11 < SB_HEADS:
                    stick_sp(layer, i - 11)
                if i >= 14 and (i - 14) % 2 == 0 and (i - 14) // 2 < 4:
                    stick_out(layer, (i - 14) // 2)
                if i == 3:
                    glu(layer, 0)
                if i == 5:
                    glu(layer, 1)
                if 4 <= i < 26:
                    taps(layer, i)
                if i == 26:
                    dve.wait_ge(conv_taps, tap_count[0])
                    dve.sem_inc(conv_done, 1)
                if i == 21:
                    gla_cum(layer)
                if i == 22:
                    gla_decay(layer)
                if i == 25:
                    gla_states(layer)
                if i == 27:
                    gla_scale(layer)
                    dve.wait_ge(mean_copied, layer + 1)
                    dve.tensor_tensor(conv_acc, conv_acc, bcast(rt, 4), ALU.subtract).then_inc(centred, 1)
                if i == 29:
                    dve.wait_ge(centred, layer + 1)
                    dve.wait_ge(cv_root, layer + 1)
                    link(dve.reciprocal(rs, rt))
                    dve.tensor_tensor(conv_acc, conv_acc, bcast(rs, 4), ALU.mult).then_inc(cv_scaled, 1)
                if i == 30:
                    dve.wait_ge(consumed, WPOS["z", layer, 27, 0] + 1)
                    dve.wait_ge(cv_silu, 4 * (layer + 1))
                    split(br_hi[0], br_lo[0], conv_tmp, a_split, layer + 1)
                if i == 32:
                    dve.wait_ge(gg_silu, layer + 1)
                    link(dve.tensor_tensor(gla_o, gla_o, gg, ALU.mult))
                    split(br_hi[2], br_lo[2], gla_o, c_split, layer + 1)
                if i in (36, 37):
                    for q in (2 * i - 72, 2 * i - 71):
                        dve.wait_ge(merged_hi, 4 * layer + q + 1)
                        dve.tensor_tensor(h_lo[:, 2 * q:2 * q + 2, :], merged[:, 2 * q:2 * q + 2, :],
                                          f32(h_hi[:, 2 * q:2 * q + 2, :]), ALU.subtract).then_inc(s_split, 1)

            def mixer_out(layer):
                for j in range(4):
                    wait_read(dve, ("wo", layer, j, 0))
                norm_out(y, layer, P_M, 2 * layer + 1)

            dve.wait_ge(cond_ready, 1)
            order = iter(PLAN)

            def take(u):
                for v in order:
                    if v[0] == "ada":
                        add_ada(v)
                    else:
                        assert v == u
                        write_lo(u)
                        return
                    if v == first_group:
                        reciprocal_rms()

            first_group = ("ada", 0, 0, KC - 2)

            for layer in range(DEPTH):
                units = mixer_units(layer)
                for i in range(len(units)):
                    if layer and i == 1:
                        dve.wait_ge(down_copied, 4)
                        norm_out(y, 0, P_F, 2 * layer)
                    for j in ahead(i, len(units)):
                        take(units[j])
                    if i >= LAG and units[i - LAG][0] == "out":
                        merge(layer, i - LAG, units[i - LAG])
                    hook(layer, i)
                if layer == 0:
                    for i, u in enumerate(FFN_UNITS):
                        if i == 1:
                            mixer_out(layer)
                        take(u)
                        if i == 1:
                            norm_in(layer, A_F, 2 * layer + 2)
                        if i >= LAG and FFN_UNITS[i - LAG][0] == "up":
                            b = FFN_UNITS[i - LAG]
                            t = b[2]
                            wait_read(dve, ("gate", 0, t, 0))
                            dve.wait_ge(consumed, WPOS[b] + 1)
                            bk, before = BANKS[b][0]
                            dve.tensor_tensor(prod[t % 2], two(bank[bk]), silu_g[t % 2],
                                              ALU.mult).then_inc(bank_read[bk], 1)
                            dve.wait_ge(bank_read[bk], before + 1)
                            split(ff_hi[t % 2], ff_lo[t % 2], prod[t % 2], ff_split, t + 1)
                        for g, t in enumerate(ADA_TURN):
                            if u == ("up", 0, t, 0):
                                finish_mods(1, g)
                else:
                    mixer_out(layer)
                    norm_in(layer, A_F, 2 * layer + 2, split_too=False)

            dve.wait_ge(moe_consts, 3)
            dve.wait_ge(logits_done, 1)
            link(dve.tensor_copy(logits, Z[0][:, 0:16]))
            for t in range(2):
                lg = logits[:, 8 * t:8 * t + 8]
                link(dve.max(top[:, t, :], lg))
                link(dve.max_index(index[:, t, :], top[:, t, :], lg))
                link(dve.tensor_copy(index_f[:, t, :], index[:, t, :]))
                link(dve.tensor_tensor(prob[:, t, 0:1], top[:, t, 1:2], top[:, t, 0:1], ALU.subtract))
            dve.sem_inc(gap_ready, 1)
            dve.wait_ge(exp_done, 1)
            link(dve.tensor_scalar(prob[:, :, 0], prob[:, :, 1], 1.0, None, ALU.add))
            link(dve.reciprocal(prob[:, :, 0], prob[:, :, 0]))
            link(dve.tensor_tensor(prob[:, :, 1], prob[:, :, 1], prob[:, :, 0], ALU.mult))
            for t in range(2):
                link(dve.tensor_scalar(pick[:, t, :], iota8, index_f[:, t, 0:1], None, ALU.is_equal))
                link(dve.tensor_scalar(pick2[:, t, :], iota8, index_f[:, t, 1:2], None, ALU.is_equal))
                link(dve.tensor_scalar(comb[:, t, :], pick[:, t, :], prob[:, t, 0:1], None, ALU.mult))
                link(dve.scalar_tensor_tensor(comb[:, t, :], pick2[:, t, :], prob[:, t, 1:2],
                                              comb[:, t, :], ALU.mult, ALU.add))
                link(dve.tensor_tensor(pick[:, t, :], pick[:, t, :], pick2[:, t, :], ALU.add))
            dve.sem_inc(routed, 1)
            dve.wait_ge(counted, 1)
            for t in range(2):
                r = Z[0][:, 16 + 8 * t:24 + 8 * t]
                link(dve.tensor_copy(places[:, t, 0:8], r))
                link(dve.tensor_scalar(places[:, t, 8:16], r, float(P), None, ALU.subtract))
                for i in range(2):
                    link(dve.tensor_copy(chosen[:, t, 8 * i:8 * i + 8], pick[:, t, :]))
                    link(dve.tensor_copy(weights[:, t, 8 * i:8 * i + 8], comb[:, t, :]))
            link(dve.tensor_scalar(over, Z[0][:, 32:40], float(P), None, ALU.is_gt))
            link(dve.tensor_tensor_scan(place8, ones[:, 0:8], over, 0.0, ALU.mult, ALU.add))
            link(dve.tensor_copy(list_f[:, 0:1], place8[:, 7:8]))
            for j in range(3):
                link(dve.scalar_tensor_tensor(hits, place8, float(j + 1), over, ALU.is_equal, ALU.mult))
                link(dve.tensor_tensor(hits, hits, iota8, ALU.mult))
                link(dve.reduce_sum(list_f[:, j + 1:j + 2], hits, mybir.AxisListType.X))
            link(dve.tensor_copy(ints[:, 0:4], list_f[:, 0:4]))
            link(dve.tensor_copy(column_f[:, 0:8], iota8))
            link(dve.memset(column_f[:, 8:12], 0.0))
            link(dve.tensor_scalar(column_f[:, 8:11], list_f[:, 1:4], float(N_EXP), None, ALU.add))
            link(dve.tensor_copy(ints[:, 8:20], column_f))
            dve.sem_inc(list_ready, 1)
            link(dve.memset(moe_y, 0.0))
            dve.memset(sel_w, 0.0).then_inc(sel_zeroed, 1)

            def moe_lo(step, k, rounds=0):
                slot, _, s, w = moe_unit(step, k, rounds)
                dve.wait_ge(hi_written, w + 1)
                dve.tensor_tensor(w_lo[s], raw[:, slot, :], f32(w_hi[s]),
                                  ALU.subtract).then_inc(lo_written, 1)
                dve.wait_ge(lo_written, w + 1)
                dve.sem_inc(released, 1)

            def multiply(step, k, odd, t, rounds=0):
                dve.wait_ge(silu_done, step * FT + t + 1)
                dve.wait_ge(consumed, moe_unit(step, k, rounds)[3] + 1)
                dve.tensor_tensor(act_e[odd], bank[2 * odd + 1][:, :], silu_e[odd],
                                  ALU.mult).then_inc(act_done, 1)

            def split_tile(step, odd, t):
                dve.wait_ge(turned, step * FT + t + 1)
                dve.tensor_copy(ae_hi[odd], bank[4][:, :]).then_inc(ae_hi_done, 1)
                dve.wait_ge(ae_hi_done, step * FT + t + 1)
                dve.tensor_tensor(ae_lo[odd], bank[4][:, :], f32(ae_hi[odd]), ALU.subtract).then_inc(ae_split, 1)

            def select(step, to, w, ready):
                column = dve.value_load(ints[0:1, bass.ds(step + 8, 1)], min_val=0, max_val=15)
                for t in range(2):
                    col = bass.ds(column + 16 * t, 1)
                    dve.tensor_scalar(to[:, P * t:P * t + P], iota, places_f[:, col], w[:, col],
                                      ALU.is_equal, ALU.mult).then_inc(ready, 1)

            def split_input(step, half):
                dve.wait_ge(gathered, step * 2 + half + 1)
                src = (bank[7], bank[4])[half]
                c = 512 * half
                dve.tensor_copy(xe_hi[:, c:c + 512], src[:, :]).then_inc(xe_hi_done, 1)
                dve.wait_ge(xe_hi_done, step * 2 + half + 1)
                dve.tensor_tensor(xe_lo[:, c:c + 512], src[:, :], f32(xe_hi[:, c:c + 512]),
                                  ALU.subtract).then_inc(xe_split, 1)

            def add_result(step):
                for p in range(4):
                    dve.wait_ge(scattered, step * 4 + p + 1)
                    to = moe_y[:, 512 * p:512 * p + 512]
                    dve.tensor_tensor(to, to, SCATTER[p][:, :], ALU.add).then_inc(moe_added, 1)

            def expert_step(step, expert):
                for k in range(4):
                    moe_lo(step, k)
                add_result(step)
                dve.wait_ge(sel_turned, step + 1)
                select(step, sel_w, weights_f, sel_w_ready)
                multiply(step, 3, 0, 0)
                with dve.Fori(0, (FT - 1) // 2) as q:
                    for r in range(2):
                        t = q * 2 + (1 + r)
                        moe_lo(step, 4 + 6 * r, q * 2)
                        split_tile(step, r, t - 1)
                        for j in range(1, 6):
                            moe_lo(step, 4 + 6 * r + j, q * 2)
                        multiply(step, 4 + 6 * r + 3, 1 - r, t, q * 2)
                select(step + 1, sel, chosen_f, sel_ready)
                split_tile(step, 0, FT - 1)
                for half in range(2):
                    moe_lo(step, EU - 2 + half)
                    split_input(step + 1, half)

            select(0, sel, chosen_f, sel_ready)
            for half in range(2):
                split_input(0, half)
            with dve.Fori(0, N_EXP) as g:
                expert_step(g, g)
            add_result(over_steps(dve, expert_step))
            norm_out(area(A_GATES + 2048, KC, T), 1, P_F, 2 * DEPTH)

        @block.tensor
        def _(pe):
            norms = [0]
            pe.wait_ge(consts, 5)

            def parts(w, slot):
                return ((w_hi[slot], True), (w_hi[slot], False), (w_lo[slot], True))

            def reduce_mods(layer, g):
                pe.wait_ge(ada_summed, 3 * layer + g + 1)
                acc = ada_acc[layer, g]
                for c in range(16):
                    mm = pe.matmul(M[:, 16 * g + c:16 * g + c + 1], acc[:, P * c:P * c + P], ones[:, 0:1],
                                   start=True, stop=True)
                mm.then_inc(ada_reduced, 1)

            def norm_sums(first=0, last=4, squares=squares, sums=M):
                for q in range(first, last):
                    pe.wait_ge(norm_squares, 4 * norms[0] + q + 1)
                    for c in (2 * q, 2 * q + 1):
                        mm = pe.matmul(sums[:, 0:T], ones, squares[:, c, :], start=(c == 0), stop=(c == KC - 1),
                                       skip_group_check=True)
                if last == 4:
                    mm.then_inc(norm_sum, 1)
                    norms[0] += 1

            def begin(u):
                pe.wait_ge(lo_written, WPOS[u] + 1)
                for b, before in BANKS[u]:
                    if before:
                        pe.wait_ge(bank_read[b], before)
                return SLOT[u]

            def project(u, hi, lo, ready=None, before=0, chunks=1):
                s = begin(u)
                out = two(bank[BANKS[u][0][0]])
                for k in range(KC):
                    if ready is not None:
                        pe.wait_ge(ready, before + k // chunks + 1)
                    for c in range(2):
                        for n, (w, high) in enumerate(parts(u, s)):
                            mm = pe.matmul(out[:, c, :], w[:, 256 * k + P * c:256 * k + P * c + P],
                                           (hi if high else lo)[:, k, :],
                                           start=(k == 0 and n == 0 and c == 0),
                                           stop=(k == KC - 1 and n == 2), skip_group_check=True)
                mm.then_inc(consumed, 1)

            def project_tokens(u, hi, lo):
                s = begin(u)
                out = two(bank[BANKS[u][0][0]])
                for t in range(2):
                    for k in range(KC):
                        for n, (w, high) in enumerate(parts(u, s)):
                            mm = pe.matmul(out[:, t, :], (hi if high else lo)[:, k, P * t:P * t + P],
                                           w[:, 256 * k:256 * k + 256],
                                           start=(k == 0 and n == 0), stop=(k == KC - 1 and n == 2))
                mm.then_inc(consumed, 1)

            def project_branch(u, hi, lo):
                s = begin(u)
                for c in range(4):
                    out = two(bank[BANKS[u][c // 2][0]])
                    for k in range(4):
                        for n, (w, high) in enumerate(parts(u, s)):
                            mm = pe.matmul(out[:, c % 2, :], w[:, 512 * k + P * c:512 * k + P * c + P],
                                           (hi if high else lo)[:, k, :],
                                           start=(k == 0 and n == 0), stop=(k == 3 and n == 2))
                mm.then_inc(consumed, 1)

            def project_down(u):
                t = u[2]
                pe.wait_ge(ff_split, t + 1)
                s = begin(u)
                for f in range(2):
                    for c in range(KC):
                        out = two(FB[c // 2])
                        for n, (w, high) in enumerate(parts(u, s)):
                            first = t == 0 and f == 0 and n == 0 and c % 2 == 0
                            last = t == PAIRS - 1 and f == 1 and n == 2
                            mm = pe.matmul(out[:, c % 2, :], w[:, 1024 * f + P * c:1024 * f + P * c + P],
                                           (ff_hi if high else ff_lo)[t % 2][:, f, :],
                                           start=first, stop=last, skip_group_check=True)
                mm.then_inc(consumed, 1)

            def stick_z(layer, hh):
                n, c, p = layer * SB_HEADS + hh, hh // 2, 64 * (hh % 2)
                if hh >= 2:
                    pe.wait_ge(att_ready, n - 1)
                q, k = sq[p:p + 64, c, :], sk[p:p + 64, c, :]
                pe.matmul(Z[hh % 2][:, 0:T], k[:, 0:P], q, start=True, stop=False, skip_group_check=True)
                pe.matmul(Z[hh % 2][:, T:T + P], k[:, P:T], q[:, P:T], start=False, stop=False,
                          skip_group_check=True).then_inc(z_ready, 1)

            def stick_sum(layer, hh):
                z, s = Z[hh % 2], flat(stick_s[hh % 2])
                pe.wait_ge(sp_masked, layer * SB_HEADS + hh + 1)
                pe.matmul(z[:, 0:T], l_neg, s[:, 0:T], start=False, stop=False, skip_group_check=True)
                pe.matmul(z[:, P:T], neg, s[:, T:T + P], start=False, stop=False, skip_group_check=True)
                pe.matmul(z[:, T:T + P], l_neg, s[:, T:T + P], start=False, stop=True,
                          skip_group_check=True).then_inc(arg_ready, 1)

            def stick_o(layer, hh):
                n, c, p = layer * SB_HEADS + hh, hh // 2, 64 * (hh % 2)
                if c >= 2 and hh % 2 == 0:
                    pe.wait_ge(o_split, 4 * layer + c - 1)
                pe.wait_ge(att_masked, n + 1)
                e = flat(stick_e[hh % 2])
                out = O[c % 2][p:p + 64, :]
                pe.matmul(out[:, 0:T], sv[:, 0, 64 * hh:64 * hh + 64], e[:, 0:T], start=True, stop=False,
                          skip_group_check=True)
                pe.matmul(out[:, P:T], sv[:, 1, 64 * hh:64 * hh + 64], e[:, T:T + P], start=False, stop=True,
                          skip_group_check=True).then_inc(o_ready, 1)

            def low_rank(layer):
                pe.wait_ge(lr_loaded, 32 * (layer + 1))
                pe.wait_ge(norm_root, norms[0])
                for k in range(KC):
                    mm = pe.matmul(M[0:RANK, 0:T], wglr[:, k, :], hf[:, k, :], start=(k == 0),
                                   stop=(k == KC - 1))
                mm.then_inc(lr_ready, 1)

            def log_a(layer, half):
                if half:
                    pe.wait_ge(la_read, 8 * layer + 4)
                else:
                    pe.wait_ge(lr_copied, 2 * (layer + 1))
                    pe.wait_ge(mods_ready, 2)
                for k in range(2):
                    h = 2 * half + k
                    mm = pe.matmul(M[:, T * k:T * k + T], a2_sb[0:RANK, P * h:P * h + P], glr[0:RANK, :],
                                   start=True, stop=True)
                mm.then_inc(la_ready, 1)

            def gla_turn(layer):
                pe.wait_ge(dec_ready, layer + 1)
                pe.wait_ge(o_split, 4 * (layer + 1))
                for t in range(2):
                    for h in range(GLA_HEADS):
                        mm = pe.transpose(Z[t][:, P * h:P * h + P], gap[:, h, P * t:P * t + P], ident)
                    mm.then_inc(ke_ready, 1)
                for t in range(2):
                    for h in range(GLA_HEADS):
                        mm = pe.matmul(O[t][:, P * h:P * h + P], e_out[:, h, P * t:P * t + P],
                                       e_in[:, h, P * t:P * t + P], start=True, stop=True)
                    mm.then_inc(sc_ready, 1)

            def gla_states(layer):
                pe.wait_ge(ke_copied, 2 * (layer + 1))
                pe.wait_ge(la_read, 8 * (layer + 1))
                pe.wait_ge(mods_ready, 3)
                for j in range(3):
                    p, t = CH * (j % 2), j // 2
                    for h in range(GLA_HEADS):
                        mm = pe.matmul((M, Z[0], Z[1])[j][:, P * h:P * h + P],
                                       ket[p:p + CH, 512 * t + P * h:512 * t + P * h + P],
                                       gv[p:p + CH, t, P * h:P * h + P], start=True, stop=True)
                    mm.then_inc(ds_ready, 1)

            def gla_out(layer):
                pe.wait_ge(st_ready, layer + 1)
                pe.wait_ge(sc_masked, layer + 1)
                for h in range(GLA_HEADS):
                    out = two(O[h // 2])[:, h % 2, :]
                    for t in range(2):
                        pe.matmul(out[:, P * t:P * t + P], gv[:, t, P * h:P * h + P],
                                  s_t[:, 512 * t + P * h:512 * t + P * h + P], start=(t == 0), stop=False,
                                  skip_group_check=True)
                    for j in range(1, 4):
                        mm = pe.matmul(out[:, CH * j:CH * j + CH], states[j - 1][:, P * h:P * h + P],
                                       e_in[:, h, CH * j:CH * j + CH], start=False, stop=(j == 3),
                                       skip_group_check=True)
                    if h % 2:
                        mm.then_inc(go_ready, 1)

            def gla_sums(layer):
                pe.wait_ge(go_copied, 4 * (layer + 1))
                for t in range(2):
                    pe.matmul((M, Z[0])[t][:, :], ones, area(A_ST + 512 * t, 512), start=True,
                              stop=True).then_inc(gs_ready, 1)

            def conv_sums(layer, src, ready, value, done):
                pe.wait_ge(ready, value)
                pe.wait_ge(pool_taps, TAPS * (layer + 1))
                for c in range(4):
                    mm = pe.matmul(Z[1][:, 0:T], ones, src[:, c, :], start=(c == 0), stop=(c == 3))
                mm.then_inc(done, 1)

            def hook(layer, i):
                if i == 0:
                    low_rank(layer)
                if layer == 0 and i == 10:
                    pe.wait_ge(lr_copied, 2)
                    reduce_mods(0, 1)
                if layer == 0 and i == 22:
                    pe.wait_ge(la_read, 8)
                    reduce_mods(0, 2)
                if 0 <= i - 12 < SB_HEADS:
                    stick_o(layer, i - 12)
                if 0 <= i - 11 < SB_HEADS:
                    stick_sum(layer, i - 11)
                if 0 <= i - 10 < SB_HEADS:
                    if i == 10:
                        wait_read(pe, ("z", layer, 7, 0))
                    if i == 12:
                        wait_read(pe, ("z", layer, 9, 0))
                    stick_z(layer, i - 10)
                if i == 19:
                    log_a(layer, 0)
                if i == 20:
                    log_a(layer, 1)
                if i == 23:
                    gla_turn(layer)
                if i == 24:
                    gla_states(layer)
                if i == 25:
                    gla_out(layer)
                if i == 26:
                    gla_sums(layer)
                    conv_sums(layer, conv_acc, conv_done, layer + 1, mean_ready)
                if i == 28:
                    conv_sums(layer, conv_tmp, cv_squared, layer + 1, var_ready)

            norm_sums()
            pe.wait_ge(norm_root, 1)
            reduce_mods(0, 0)
            for layer in range(DEPTH):
                if layer:
                    pe.wait_ge(mods_ready, 6)
                    norm_sums()
                    norm_sums()
                for i, u in enumerate(mixer_units(layer)):
                    if i == 0:
                        project(u, h_hi, h_lo, h_split, 2 * layer * KC)
                    elif u[0] == "z":
                        (project_tokens if z_columns()[u[2]][1] else project)(u, h_hi, h_lo)
                    elif u[0] == "out":
                        b = u[2]
                        if b == 0:
                            pe.wait_ge(a_split, layer + 1)
                        if b == 2:
                            pe.wait_ge(c_split, layer + 1)
                        if i == 32:
                            pe.wait_ge(cv_root, layer + 1)
                        project_branch(u, br_hi[b], br_lo[b])
                    elif u[2] == 0:
                        project(u, h_hi, h_lo, s_split, 4 * layer, 2)
                    else:
                        project(u, h_hi, h_lo)
                    hook(layer, i)
                    if i == 38:
                        norm_sums(0, 1)
                norm_sums(1, 4)
                norm_sums()
                if layer == 0:
                    for i, u in enumerate(FFN_UNITS):
                        if u[0] == "down":
                            project_down(u)
                        elif i == 0:
                            project(u, h_hi, h_lo, h_split, KC)
                        else:
                            project(u, h_hi, h_lo)
                        for g, t in enumerate(ADA_TURN):
                            if u == ("gate", 0, t, 0):
                                if g:
                                    pe.wait_ge(mods_ready, 3 + g)
                                reduce_mods(1, g)

            pe.wait_ge(router_loaded, 16)
            pe.wait_ge(h_ready, 4 * KC)
            for t in range(2):
                for k in range(KC):
                    mm = pe.matmul(Z[0][:, 8 * t:8 * t + 8], hf[:, k, P * t:P * t + P], router_sb[:, k, :],
                                   start=(k == 0), stop=(k == KC - 1))
            mm.then_inc(logits_done, 1)
            for q in range(4):
                t, half = divmod(q, 2)
                for c in range(4):
                    mm = pe.transpose((O[0], O[1], M, Z[1])[q][:, P * c:P * c + P],
                                      hf[:, 4 * half + c, P * t:P * t + P], ident)
                mm.then_inc(htok_turned, 1)
            pe.wait_ge(routed, 1)
            pe.matmul(Z[0][:, 16:24], tril, pick_f[:, 0:8], start=True, stop=True)
            pe.matmul(Z[0][:, 24:32], ones, pick_f[:, 0:8], start=True, stop=False)
            pe.matmul(Z[0][:, 24:32], tril, pick_f[:, 8:16], start=False, stop=True)
            pe.matmul(Z[0][:, 32:40], ones, pick_f[:, 0:8], start=True, stop=False)
            pe.matmul(Z[0][:, 32:40], ones, pick_f[:, 8:16], start=False, stop=True).then_inc(counted, 1)
            pe.wait_ge(htok_copied, 4)
            pe.wait_ge(sel_zeroed, 1)

            def moe_begin(step, k, rounds=0):
                _, _, s, w = moe_unit(step, k, rounds)
                pe.wait_ge(lo_written, w + 1)
                return s

            def gate_up(step, k, b, half, rounds=0):
                s = moe_begin(step, k, rounds)
                for kk in range(4):
                    c = P * (4 * half + kk)
                    for n, (w, high) in enumerate(parts(None, s)):
                        mm = pe.matmul(bank[b][:, :], (xe_hi if high else xe_lo)[:, c:c + P],
                                       w[:, 512 * kk:512 * kk + 512],
                                       start=(half == 0 and kk == 0 and n == 0),
                                       stop=(half == 1 and kk == 3 and n == 2))
                mm.then_inc(consumed, 1)

            def down(step, k, odd, half, t, first=False, last=False, rounds=0):
                if half == 0:
                    pe.wait_ge(ae_split, step * FT + t + 1)
                s = moe_begin(step, k, rounds)
                for f in range(2):
                    c = P * (2 * half + f)
                    for d in range(2):
                        for n, (w, high) in enumerate(parts(None, s)):
                            mm = pe.matmul(bank[5 + d][:, :], (ae_hi if high else ae_lo)[odd][:, c:c + P],
                                           w[:, 1024 * f + 512 * d:1024 * f + 512 * d + 512],
                                           start=(first and half == 0 and f == 0 and n == 0),
                                           stop=(last and half == 1 and f == 1 and n == 2),
                                           skip_group_check=True)
                mm.then_inc(consumed, 1)

            def turn(step, odd, t):
                pe.wait_ge(act_done, step * FT + t + 1)
                for c in range(4):
                    mm = pe.transpose(bank[4][:, P * c:P * c + P], act_e[odd][:, P * c:P * c + P], ident)
                mm.then_inc(turned, 1)

            def gather(step, half):
                if half == 0:
                    pe.wait_ge(sel_ready, step * 2 + 2)
                for c in range(4):
                    for t in range(2):
                        at = D * t + P * (4 * half + c)
                        mm = pe.matmul((bank[7], bank[4])[half][:, P * c:P * c + P],
                                       h_tok[:, at:at + P], sel[:, P * t:P * t + P],
                                       start=(t == 0), stop=(t == 1))
                mm.then_inc(gathered, 1)

            def turn_selection():
                for t in range(2):
                    mm = pe.transpose(bank[7][:, P * t:P * t + P], sel_w[:, P * t:P * t + P], ident)
                mm.then_inc(sel_turned, 1)

            def scatter(step):
                pe.wait_ge(ye_copied, step * 3 + 3)
                pe.wait_ge(xe_split, step * 2 + 2)
                for p in range(4):
                    for c in range(2):
                        d = P * (2 * p + c)
                        mm = pe.matmul(SCATTER[p][:, T * c:T * c + T], y_e[:, d:d + P], sel_t,
                                       start=True, stop=True)
                    mm.then_inc(scattered, 1)

            def expert_step(step, expert):
                pe.wait_ge(xe_split, step * 2 + 2)
                for k in range(2):
                    gate_up(step, k, 0, k)
                scatter(step)
                for k in range(2):
                    gate_up(step, 2 + k, 1, k)
                pe.wait_ge(moe_added, step * 4 + 4)
                turn(step, 0, 0)
                for r in range(2):
                    tile(step, r, 0, r + 1, r == 0)
                with pe.Fori(1, (FT - 1) // 2) as q:
                    for r in range(2):
                        tile(step, r, q * 2, q * 2 + (1 + r), False)
                gather(step + 1, 0)
                pe.wait_ge(ae_split, step * FT + FT)
                gather(step + 1, 1)
                for half in range(2):
                    down(step, EU - 2 + half, 0, half, FT - 1, last=True)
                pe.wait_ge(xe_split, step * 2 + 3)
                pe.wait_ge(sel_w_ready, step * 2 + 2)
                turn_selection()

            def tile(step, r, rounds, t, first):
                k, odd = 4 + 6 * r, 1 - r
                for j in range(2):
                    gate_up(step, k + j, 2 * odd, j, rounds)
                for j in range(2):
                    gate_up(step, k + 2 + j, 2 * odd + 1, j, rounds)
                down(step, k + 4, 1 - odd, 0, t - 1, first=first, rounds=rounds)
                turn(step, odd, t)
                down(step, k + 5, 1 - odd, 1, t - 1, rounds=rounds)

            gather(0, 0)
            gather(0, 1)
            pe.wait_ge(xe_split, 1)
            turn_selection()
            with pe.Fori(0, N_EXP) as g:
                expert_step(g, g)
            scatter(over_steps(pe, expert_step))
            norm_sums(squares=area(A_SQ, KC, T), sums=O[0])


def lay_out(inputs):
    f = {k: np.asarray(v) for k, v in inputs.items()}

    def channels(v):
        return v.reshape(-1, P).T

    vecs = []
    for layer in range(DEPTH):
        for name in VECS:
            if name == "conv_dw":
                w = f[name][layer].reshape(TAPS, 4, P)
                vecs.append(w.transpose(2, 1, 0).reshape(P, 4 * TAPS))
            else:
                vecs.append(channels(f[name][layer]))
    vecs.append(channels(f["c"][0]))

    def rows(w, chunks):
        return w.reshape(chunks, P, -1).transpose(1, 0, 2).reshape(P, WORDS)

    stream = np.empty((N_UNITS, P, WORDS), np.float32)
    cols = z_columns()
    branch = ("w_conv_out", "w_sb_out", "w_gla_out")
    for n, (kind, layer, a, b) in enumerate(PLAN):
        if kind == "ada":
            stream[n] = f["ada_w"][layer][P * b:P * b + P, WORDS * a:WORDS * a + WORDS]
        elif kind == "z":
            c = cols[a][0]
            stream[n] = rows(f["w_in"][layer][:, c:c + 256], KC)
        elif kind == "out":
            stream[n] = rows(f[branch[a]][layer][:, 512 * b:512 * b + 512], 4)
        elif kind == "wo":
            stream[n] = rows(f["w_o"][layer][:, 256 * a:256 * a + 256], KC)
        elif kind == "gate":
            stream[n] = rows(f["ffn_w_gate"][0][:, 256 * a:256 * a + 256], KC)
        elif kind == "up":
            stream[n] = rows(f["ffn_w_up"][0][:, 256 * a:256 * a + 256], KC)
        else:
            stream[n] = rows(f["ffn_w_down"][0][256 * a:256 * a + 256, :], 2)

    experts = np.empty((N_EXP, EU, P, WORDS), np.float32)
    for e in range(N_EXP):
        def pair(w, t):
            c = w[:, 512 * t:512 * t + 512]
            return [rows(c[512 * h:512 * h + 512], 4) for h in range(2)]

        def downs(t):
            w = f["moe_w_down"][0, e]
            return [rows(w[512 * t + 256 * h:512 * t + 256 * h + 256], 2) for h in range(2)]

        units = []
        for t in range(FT):
            units += pair(f["moe_w_gate"][0, e], t) + pair(f["moe_w_up"][0, e], t)
            if t:
                units += downs(t - 1)
        units += downs(FT - 1)
        experts[e] = units

    def turned(v):
        return v.T.reshape(KC, P, T).transpose(1, 0, 2)

    return {
        "x_t": turned(f["x"][0]),
        "vecs": np.concatenate(vecs, axis=1),
        "glr_w": f["w_in"][:, :, O_LR:O_LR + RANK].reshape(DEPTH, KC, P, RANK).transpose(0, 2, 1, 3),
        "a2": f["gla_a2"],
        "router": f["router_w"][0].reshape(KC, P, N_EXP).transpose(1, 0, 2),
        "stream": stream,
        "experts": experts.reshape(N_EXP * EU, P, WORDS),
    }


def kernel(**inputs):
    import concourse.bacc as bacc
    from concourse.bass_utils import run_bass_kernel_spmd

    nc = bacc.Bacc("TRN2", target_bir_lowering=False, num_devices=1)
    arrays, args = {}, {}
    for name, a in lay_out(inputs).items():
        a = np.ascontiguousarray(a)
        arrays[f"in_{name}"] = a
        args[name] = nc.dram_tensor(f"in_{name}", a.shape, mybir.dt.from_np(a.dtype), kind="ExternalInput").ap()
    args["out_t"] = nc.dram_tensor("out_t", (P, KC, T), F32, kind="ExternalOutput").ap()
    program(nc, **args)
    result = run_bass_kernel_spmd(nc, [arrays], core_ids=[0]).results[0]["out_t"]
    return np.ascontiguousarray(result.transpose(1, 0, 2).reshape(D, T).T)[None]
```
